# Optimizing a Trainium2 kernel written in Bass

```python
import math
import jax, jax.numpy as jnp
from jax import lax
import numpy as np

D_MODEL = 1024
BATCH = 1
SEQ = 128
DEPTH = 1
DEC_BATCH = 1
DEC_SEQ = 1024
PAST_LEN = 256

GRID_W = 64
CONV_CH = D_MODEL
CONV_W = 31
CONV_PAD = CONV_W // 2
RET_HEADS = 4
RET_DK = 256
RET_DV = 512
RET_QK_W = RET_HEADS * RET_DK
RET_V_W = RET_HEADS * RET_DV
CHUNK = 128
MLP_W = 4 * D_MODEL
PROJ_W = 2 * CONV_CH + 2 * RET_QK_W + 2 * RET_V_W + 2 * D_MODEL
ROPE_BASE = 10000.0
EPS = 1e-6

kernel_name = "hybrid_conformer_retention_dit_step"

def _rmsnorm(x, g):
    xf = x.astype(jnp.float32)
    y = xf * lax.rsqrt(jnp.mean(xf * xf, axis=-1, keepdims=True) + EPS)
    return (y * g.astype(jnp.float32)).astype(x.dtype)

def _head_norm(y):
    yf = y.astype(jnp.float32)
    mu = jnp.mean(yf, axis=-1, keepdims=True)
    var = jnp.mean(jnp.square(yf - mu), axis=-1, keepdims=True)
    return ((yf - mu) * lax.rsqrt(var + EPS)).astype(y.dtype)

def _rope_2d(x):
    L = x.shape[1]
    t = jnp.arange(L)
    row = (t // GRID_W).astype(jnp.float32)
    col = (t % GRID_W).astype(jnp.float32)
    nf = RET_DK // 4
    inv = ROPE_BASE ** (-jnp.arange(nf, dtype=jnp.float32) / nf)
    ang = jnp.concatenate([row[:, None] * inv, col[:, None] * inv], axis=-1)[None, :, None, :]
    cos = jnp.cos(ang).astype(x.dtype)
    sin = jnp.sin(ang).astype(x.dtype)
    x1, x2 = jnp.split(x, 2, axis=-1)
    return jnp.concatenate([x1 * cos - x2 * sin, x2 * cos + x1 * sin], axis=-1)

def _dwconv(u, w, b):
    out = lax.conv_general_dilated(
        u, w[:, None, :].astype(u.dtype), window_strides=(1,), padding=[(CONV_PAD, CONV_PAD)],
        dimension_numbers=("NWC", "WIO", "NWC"), feature_group_count=u.shape[-1])
    return out + b.astype(u.dtype)

def _retention_scan(q, k, v, log_gamma, s0):
    B, L, H, DK = q.shape
    DV = v.shape[-1]
    n = L // CHUNK
    dt = q.dtype
    lg = log_gamma.astype(jnp.float32)
    idx = jnp.arange(CHUNK, dtype=jnp.float32)
    diff = idx[:, None] - idx[None, :]
    dmat = jnp.where(diff[None] >= 0, jnp.exp(jnp.maximum(diff, 0.0)[None] * lg[:, None, None]), 0.0).astype(dt)
    q_dec = jnp.exp((idx + 1.0)[:, None] * lg[None, :]).astype(dt)
    k_dec = jnp.exp((CHUNK - 1.0 - idx)[:, None] * lg[None, :]).astype(dt)
    s_dec = jnp.exp(CHUNK * lg).astype(dt)

    def chunks(t):
        return jnp.moveaxis(t.reshape(B, n, CHUNK, H, t.shape[-1]), 1, 0)

    def step(s, inp):
        qc, kc, vc = inp
        scores = jnp.einsum("bihd,bjhd->bhij", qc, kc) * dmat
        y = (jnp.einsum("bhij,bjhe->bihe", scores, vc)
             + jnp.einsum("bihd,bhde->bihe", qc, s) * q_dec[None, :, :, None])
        s = s * s_dec[None, :, None, None] + jnp.einsum("bjhd,bjhe->bhde", kc * k_dec[None, :, :, None], vc)
        return s, y

    s_fin, ys = lax.scan(step, s0.astype(dt), (chunks(q), chunks(k), chunks(v)))
    y = jnp.moveaxis(ys, 0, 1).reshape(B, L, H, DV)
    return y, s_fin

def _layer(x, mod, s0, grid, norm1_g, norm2_g, w_in, conv_dw, conv_b, conv_norm_g, w_conv_out,
           decay_logit, w_ret_out, w_out, w_mlp1, w_mlp2):
    B, L, _ = x.shape
    sh1, sc1, g1, sh2, sc2, g2 = jnp.split(mod[:, None, :].astype(x.dtype), 6, axis=-1)
    h = _rmsnorm(x, norm1_g) * (1.0 + sc1) + sh1
    split_idx = [2 * CONV_CH, 2 * CONV_CH + RET_QK_W, 2 * CONV_CH + 2 * RET_QK_W,
                 2 * CONV_CH + 2 * RET_QK_W + RET_V_W, 2 * CONV_CH + 2 * RET_QK_W + 2 * RET_V_W]
    u, q, k, v, rg, bg = jnp.split(h @ w_in, split_idx, axis=-1)

    a = u[..., :CONV_CH] * jax.nn.sigmoid(u[..., CONV_CH:])
    if grid:
        rows = L // GRID_W
        a = _dwconv(a.reshape(B * rows, GRID_W, CONV_CH), conv_dw, conv_b).reshape(B, L, CONV_CH)
    else:
        a = _dwconv(a, conv_dw, conv_b)
    a = jax.nn.silu(_rmsnorm(a, conv_norm_g)) @ w_conv_out

    q = q.reshape(B, L, RET_HEADS, RET_DK)
    k = k.reshape(B, L, RET_HEADS, RET_DK) * (RET_DK ** -0.5)
    v = v.reshape(B, L, RET_HEADS, RET_DV)
    if grid:
        q = _rope_2d(q)
        k = _rope_2d(k)
    log_g = jax.nn.log_sigmoid(decay_logit.astype(jnp.float32))
    y_f, s_f = _retention_scan(q, k, v, log_g[0], s0[:, 0])
    y_b, s_b = _retention_scan(q[:, ::-1], k[:, ::-1], v[:, ::-1], log_g[1], s0[:, 1])
    y = _head_norm(y_f + y_b[:, ::-1]).reshape(B, L, RET_V_W)
    b = (jax.nn.silu(rg) * y) @ w_ret_out

    ga, gb = jnp.split(jax.nn.sigmoid(bg), 2, axis=-1)
    x = x + g1 * ((ga * a + gb * b) @ w_out)

    h2 = _rmsnorm(x, norm2_g) * (1.0 + sc2) + sh2
    x = x + g2 * (jnp.square(jax.nn.relu(h2 @ w_mlp1)) @ w_mlp2)
    return x, jnp.stack([s_f, s_b], axis=1)

def setup_inputs(seed: int = 0) -> dict:
    key = jax.random.key(seed)
    ks = jax.random.split(key, 24)
    f32 = jnp.float32

    def nrm(k, shape, scale):
        return jax.random.normal(k, shape, f32) * scale

    base_logit = jnp.log(2.0 ** (5.0 + jnp.arange(RET_HEADS, dtype=f32)) - 1.0)
    return {
        "x_prompt": nrm(ks[0], (BATCH, SEQ, D_MODEL), 1.0),
        "x_sample": nrm(ks[1], (DEC_BATCH, DEC_SEQ, D_MODEL), 1.0),
        "c": nrm(ks[2], (DEC_BATCH, D_MODEL), 1.0),
        "state_ret": nrm(ks[3], (DEC_BATCH, DEPTH, 2, RET_HEADS, RET_DK, RET_DV), 0.05),
        "c_ctx": nrm(ks[4], (D_MODEL,), 1.0),
        "norm1_g": 1.0 + nrm(ks[5], (DEPTH, D_MODEL), 0.02),
        "norm2_g": 1.0 + nrm(ks[6], (DEPTH, D_MODEL), 0.02),
        "w_mod": nrm(ks[7], (DEPTH, D_MODEL, 6 * D_MODEL), D_MODEL ** -0.5),
        "b_mod": nrm(ks[8], (DEPTH, 6 * D_MODEL), 0.02),
        "w_in": nrm(ks[9], (DEPTH, D_MODEL, PROJ_W), D_MODEL ** -0.5),
        "conv_dw": nrm(ks[10], (DEPTH, CONV_W, CONV_CH), CONV_W ** -0.5),
        "conv_b": nrm(ks[11], (DEPTH, CONV_CH), 0.02),
        "conv_norm_g": 1.0 + nrm(ks[12], (DEPTH, CONV_CH), 0.02),
        "w_conv_out": nrm(ks[13], (DEPTH, CONV_CH, D_MODEL), CONV_CH ** -0.5),
        "ret_decay_logit": base_logit[None, None, :] + nrm(ks[14], (DEPTH, 2, RET_HEADS), 0.1),
        "w_ret_out": nrm(ks[15], (DEPTH, RET_V_W, D_MODEL), RET_V_W ** -0.5),
        "w_out": nrm(ks[16], (DEPTH, D_MODEL, D_MODEL), D_MODEL ** -0.5),
        "w_mlp1": nrm(ks[17], (DEPTH, D_MODEL, MLP_W), D_MODEL ** -0.5),
        "w_mlp2": nrm(ks[18], (DEPTH, MLP_W, D_MODEL), MLP_W ** -0.5),
        "final_norm_g": 1.0 + nrm(ks[19], (D_MODEL,), 0.02),
    }

def reference(x_prompt, x_sample, c, state_ret, c_ctx, norm1_g, norm2_g, w_mod, b_mod, w_in,
              conv_dw, conv_b, conv_norm_g, w_conv_out, ret_decay_logit, w_ret_out, w_out,
              w_mlp1, w_mlp2, final_norm_g):
    xp = x_prompt
    xs = x_sample
    cond_ctx = jax.nn.silu(c_ctx)[None, :]
    cond_lat = jax.nn.silu(c)
    zero_state = jnp.zeros((xp.shape[0], 2, RET_HEADS, RET_DK, RET_DV), xp.dtype)
    new_states = []
    for l in range(DEPTH):
        lw = (norm1_g[l], norm2_g[l], w_in[l], conv_dw[l], conv_b[l], conv_norm_g[l], w_conv_out[l],
              ret_decay_logit[l], w_ret_out[l], w_out[l], w_mlp1[l], w_mlp2[l])
        mod_ctx = cond_ctx @ w_mod[l] + b_mod[l]
        xp, st = _layer(xp, mod_ctx, zero_state, False, *lw)
        new_states.append(st)
        mod_lat = cond_lat @ w_mod[l] + b_mod[l]
        xs, _ = _layer(xs, mod_lat, state_ret[:, l], True, *lw)
    new_state_ret = jnp.stack(new_states, axis=1)
    y_prompt = _rmsnorm(xp, final_norm_g)
    y_sample = _rmsnorm(xs, final_norm_g)
    return (y_prompt, y_sample, new_state_ret)


_drawn_inputs = setup_inputs


def setup_inputs(seed=0):
    import zlib

    import numpy as np

    out = dict(_drawn_inputs(seed))
    spreads = {}
    factors = {'state_ret': 200.0,
     'norm1_g': 4.45,
     'norm2_g': 9.152,
     'conv_b': 8.0,
     'conv_norm_g': 69.12,
     'final_norm_g': 19.579}
    for name, (base, spread) in spreads.items():
        noise = np.random.default_rng([zlib.crc32(name.encode()), seed]).standard_normal(out[name].shape)
        drawn = base * np.exp(spread * noise) if base else spread * noise
        out[name] = __import__('jax').numpy.asarray(drawn.astype(out[name].dtype))
    for name, factor in factors.items():
        out[name] = (out[name] * factor).astype(out[name].dtype)
    return out
```

```python
from contextlib import ExitStack

import numpy as np
import concourse.bass as bass
from concourse import mybir

F32 = mybir.dt.float32
F32R = mybir.dt.float32r
ALU = mybir.AluOpType
ACT = mybir.ActivationFunctionType

P = 128
D = 1024
KB = D // P
T = 1152
TT = T // P
G3, GN = 3, 384
H, DK, DV = 4, 256, 512
CW = 31
GRID_W = 64
NROW = 1024 // GRID_W
MLP = 4096
EPS = 1e-6
BLK = T * 4

U_V, U_QK, U_U, U_G, U_CONV, U_RET, U_OUT, U_MLP = 0, 16, 32, 48, 80, 88, 104, 112
C_U, C_Q, C_V, C_RG = 0, 2 * D, 2 * D + 2 * H * DK, 2 * D + 2 * H * DK + H * DV
V_N1, V_N2, V_CB, V_CG, V_FG, V_CC, V_C, V_BM, V_ROWS = 0, 8, 16, 24, 32, 40, 48, 56, 104
M_SH1, M_SC1, M_G1, M_SH2, M_SC2, M_G2 = 0, 8, 16, 24, 32, 40
DQ, DKK, DS = 0, 2, 4


def retention_orders():
    tiles = lambda c: (1 + 2 * c, 2 + 2 * c)
    chunk = lambda d, t: t if d == 0 else 3 - t
    norm_tiles = [3, 4, 5, 6, 1, 2, 7, 8, 0]
    pe = [("kn", 0, 0), ("kn", 1, 0)]
    for t in (0, 1):
        a, b = t, 3 - t
        pe += [("sc", a)] + [("kv", d, t, e) for d in (0, 1) for e in (0, 1)] + [("kn", 0, t + 1), ("sc", b)]
        pe += [("in", 0, t, x) for x in (0, 1)] + [("kn", 1, t + 1)] + [("ia", a, x) for x in (0, 1)]
        pe += [("in", 1, t, x) for x in (0, 1)] + [("ia", b, x) for x in (0, 1)]
    pe += [("kv", d, 2, e) for d in (0, 1) for e in (0, 1)] + [("kn", 2, 0)]
    pe += [("in", d, 2, x) for d in (0, 1) for x in (0, 1)]
    pe += [("sc", 4)] + [("in", 0, 3, x) for x in (0, 1)] + [("kv", d, 3, e) for d in (0, 1) for e in (0, 1)]
    pe += [("in", 1, 3, x) for x in (0, 1)] + [("ia", 4, 0)] + [("tr", x) for x in range(TT)]

    act = [("kh", 0), ("kh", 1)] + [("knh", d, 0, x) for d in (0, 1) for x in (0, 1)]
    act += [("vh", x) for x in range(4)] + [("qh", 0), ("qh", 1), ("ph", 0)]
    act += [("sh", d, 0, e) for d in (0, 1) for e in (0, 1)]
    act += [("sh", 0, 1, e) for e in (0, 1)] + [("knh", 0, 1, x) for x in (0, 1)] + [("ph", 3)]
    act += [("yt", 0, 0, x) for x in (0, 1)] + [("sh", 1, 1, e) for e in (0, 1)]
    act += [("vh", x) for x in range(4, 9)] + [("knh", 1, 1, x) for x in (0, 1)] + [("yt", 1, 0, x) for x in (0, 1)]
    act += [("ph", 1)] + [("sh", d, 2, e) for d in (0, 1) for e in (0, 1)] + [("knh", 0, 2, x) for x in (0, 1)]
    act += [("ph", 2)] + [("yt", 0, 1, x) for x in (0, 1)] + [("knh", 1, 2, x) for x in (0, 1)]
    act += [("yt", 1, 1, x) for x in (0, 1)]
    act += [("sh", d, 3, e) for d in (0, 1) for e in (0, 1)] + [("knh", 2, 0, x) for x in (0, 1)]
    act += [("sq", 0), ("ph", 4)] + [("so", d, e) for d in (0, 1) for e in (0, 1)] + [("yc",), ("sq", 1)]

    dve = [("dec",), ("mask",), ("kl", 0), ("kl", 1)] + [("knl", d, 0, x) for d in (0, 1) for x in (0, 1)]
    dve += [("ql", 0), ("ql", 1), ("pm", 0), ("pl", 0)] + [("su", d, 1, e) for d in (0, 1) for e in (0, 1)]
    dve += [("knl", 0, 1, x) for x in (0, 1)] + [("pm", 3), ("pl", 3)] + [("knl", 1, 1, x) for x in (0, 1)]
    dve += [("ya", c, x) for c in (0, 3) for x in (0, 1)]
    dve += [("pm", 1), ("pl", 1)] + [("su", d, 2, e) for d in (0, 1) for e in (0, 1)]
    dve += [("knl", 0, 2, x) for x in (0, 1)] + [("pm", 2), ("pl", 2)] + [("knl", 1, 2, x) for x in (0, 1)]
    dve += [("ya", c, x) for c in (1, 2) for x in (0, 1)]
    dve += [("su", d, 3, e) for d in (0, 1) for e in (0, 1)] + [("knl", 2, 0, x) for x in (0, 1)]
    dve += [("ys", d, 2, x) for d in (0, 1) for x in (0, 1)]
    dve += [("st", n) for n in range(4)] + [("pm", 4)] + [("ag", n) for n in range(4)] + [("pl", 4)]
    dve += [("ys", 0, 3, x) for x in (0, 1)] + [("ys", 1, 3, x) for x in (0, 1)]
    dve += [("st", n) for n in range(4, 9)] + [("rc", 0)] + [("ag", n) for n in range(4, 9)]
    dve += [("yn", n) for n in range(4)] + [("rc", 1)] + [("yn", n) for n in range(4, 9)] + [("gm", n) for n in range(TT)]

    pool = [("vl", x) for x in range(4)] + [("sl", d, 0, e) for d in (0, 1) for e in (0, 1)]
    pool += [("sl", 0, 1, e) for e in (0, 1)] + [("sl", 1, 1, e) for e in (0, 1)]
    pool += [("vl", x) for x in range(4, 9)]
    pool += [("sl", d, t, e) for t in (2, 3) for d in (0, 1) for e in (0, 1)]
    return tiles, chunk, norm_tiles, pe, act, dve, pool


class Order:

    def __init__(self, steps):
        self.steps, self.n, self.pos = steps, len(steps), 0
        self.at = {s: k for k, s in enumerate(steps)}
        assert len(self.at) == self.n

    def this(self, h, *step):
        return h * self.n + (self.n + self.at[step] + 1)

    def last(self, h, *step):
        return h * self.n + (self.at[step] + 1)

    def one(self, *step):
        assert self.steps[self.pos] == step, (self.steps[self.pos], step)
        self.pos += 1
        return 1


def step_kernel(nc, x_prompt, x_sample, c, state_ret, c_ctx, norm1_g, norm2_g, w_mod, b_mod, w_in,
                conv_dw, conv_b, conv_norm_g, w_conv_out, ret_decay_logit, w_ret_out, w_out,
                w_mlp1, w_mlp2, final_norm_g, t_ident, t_rope, t_coef, t_diff,
                y_prompt, y_sample, new_state):
    ctx = ExitStack()
    with ctx:
        S = lambda name: ctx.enter_context(nc.semaphore(name))
        dram = lambda name, shape: nc.dram_tensor(name, shape, F32, kind="Internal").ap()
        xT_d, conv_d = dram("xT_d", [KB, P, T]), dram("conv_d", [KB, P, T])
        qk_d, v_d = dram("qk_d", [16, P, T]), dram("v_d", [TT, P, H * DV])
        s_d, b_d, g_d = dram("s_d", [16, P, T]), dram("b_d", [16, P, T]), dram("g_d", [16, P, T])

        top = [(nc.sbuf_base + 31) // 32 * 32]

        def at(name, shape, off, dt=F32):
            return nc.alloc_sbuf_tensor_at(name, [P] + shape, dt, offset=off)

        def room(nbytes):
            off = top[0]
            top[0] += (nbytes + 31) // 32 * 32
            assert top[0] <= nc.sbuf_usable_end, (top[0], nc.sbuf_usable_end)
            return off

        ident = at("ident", [P], room(512))
        identr = at("identr", [P], room(512), F32R)
        ones = at("ones", [P], room(512))
        ones_mean = at("ones_mean", [P], room(512))
        vec = at("vec", [V_ROWS], room(416))
        cond = at("cond", [KB, 2], room(64))
        mod = at("mod", [48, 2], room(384))
        scale1 = at("scale1", [KB, 2], room(64))
        scale2 = at("scale2", [KB, 2], room(64))
        dec = at("dec", [8, 5], room(160))
        dech = at("dech", [2, 5], room(64))
        convw = at("convw", [KB, CW], room(992))
        epsc = at("epsc", [1], room(32))
        small = at("small", [64], room(256))
        ssq = at("ssq", [T], room(BLK))
        wraw = [at(f"wraw{s}", [KB, P], room(4096)) for s in (0, 1)]
        wh = [at(f"wh{s}", [KB, P], room(4096), F32R) for s in (0, 1)]
        wl = [at(f"wl{s}", [KB, P], room(4096), F32R) for s in (0, 1)]
        X0, X1, XA = room(16 * BLK), room(16 * BLK), room(8 * BLK)
        XS = room(2 * BLK)
        XEND = nc.sbuf_usable_end
        x0h, x0l = at("x0h", [KB, T], X0, F32R), at("x0l", [KB, T], X0 + 8 * BLK, F32R)
        x1h, x1l = at("x1h", [KB, T], X1, F32R), at("x1l", [KB, T], X1 + 8 * BLK, F32R)
        acc = at("acc", [KB, T], XA)
        stage = [at(f"stage{s}", [T], XS + s * BLK) for s in (0, 1)]

        B1 = X1
        vsh = [at("vs0h", [KB, 512], B1, F32R), at("vs1h", [KB, 512], B1 + 32768, F32R)]
        vsl = [at("vs0l", [KB, 512], B1 + 16384, F32R), at("vs1l", [KB, 512], B1 + 32768 + 16384, F32R)]
        wm_at = [X0 + 20480, X0 + 36864, X0 + 53248, B1, B1 + 16384]
        wmr = [at(f"wmr{s}", [KB, 256], a) for s, a in enumerate(wm_at)]
        wml = [at(f"wml{s}", [KB, 256], a, F32R) for s, a in enumerate(wm_at)]
        wmh = [at(f"wmh{s}", [KB, 256], a + 8192, F32R) for s, a in enumerate(wm_at)]
        xT = at("xT", [KB, T], B1 + 32768)
        glu = at("glu", [KB, T], B1 + 32768)
        XM = B1 + 32768 + 8 * BLK
        xnat = at("xnat", [TT, D], XM)
        rope = at("rope", [2, T], XM)
        conv_acc = at("conv_acc", [T], XM)
        conv_sq = at("conv_sq", [T], XM + BLK)
        vout = [at(f"vout{s}", [DV], XM + 2 * BLK + 2048 * s) for s in (0, 1)]
        outb = [at(f"outb{s}", [T], XM + 2 * BLK + 4096 + BLK * s) for s in (0, 1)]
        rt = at("rt", [2, T], XM + 4 * BLK + 4096)
        sa = at("sa", [T], XM + 6 * BLK + 4096)
        XK = XM + 8 * BLK
        masks = at("masks", [H, 2, 256], XK)
        XE = XK + 8192
        vrows = at("vrows", [P], XE)
        dwrows = at("dwrows", [D], X0)
        coef = at("coef", [2, 5], XE + 512)
        logit = at("logit", [8], XE + 576)
        lgt = at("lgt", [8, 8], XE + 608)
        expd = at("expd", [2, GN], B1 + 65536)
        diff0 = at("diff0", [4, GN], XM + 28672)
        assert XM + 6 * BLK + 4096 + BLK <= XM + 8 * BLK
        sqj = at("sqj", [D], X0 + 16384)
        diag = at("diag", [2, P], XE + 864)
        hb = [at(f"hb{s}", [T], XM + BLK * s) for s in (0, 1)]
        condq = at("condq", [KB, 4], XE + 1888, F32R)
        selT = at("selT", [2], XE + 2016)
        modrow = at("modrow", [2, 256], XE + 2048)
        assert XE + 2048 + 2048 <= XEND, (XE + 4096 - XEND)

        o = [X0]

        def r2(name, shape, dt=F32, n=1):
            size = (4 * int(np.prod(shape)) + 31) // 32 * 32
            if o[0] < XE and o[0] + size > XK:
                o[0] = XE
            t_ = at(name, shape, o[0], dt)
            o[0] += size
            assert o[0] <= XEND, (name, o[0], XEND)
            return t_

        kh, kl = r2("kh", [2, T], F32R), r2("kl", [2, T], F32R)
        qh, ql = r2("qh", [2, T], F32R), r2("ql", [2, T], F32R)
        vh, vl = r2("vh", [TT, DV], F32R), r2("vl", [TT, DV], F32R)
        sth = [[r2(f"sth{d}{s}", [2, DV], F32R) for s in (0, 1)] for d in (0, 1)]
        stl = [[r2(f"stl{d}{s}", [2, DV], F32R) for s in (0, 1)] for d in (0, 1)]
        sraw = [r2(f"sraw{d}", [2, DV]) for d in (0, 1)]
        knh = [r2(f"knh{d}", [2, DK], F32R) for d in (0, 1)]
        knl = [r2(f"knl{d}", [2, DK], F32R) for d in (0, 1)]
        p32 = r2("p32", [2, 256])
        ph = [r2(f"ph{s}", [2, 256], F32R) for s in (0, 1)]
        pl = [r2(f"pl{s}", [2, 256], F32R) for s in (0, 1)]
        yb = r2("yb", [TT, DV])
        maskh = r2("maskh", [2, 256])
        vst = [r2(f"vst{s}", [DV]) for s in range(3)]
        qst = [r2(f"qst{s}", [T]) for s in (0, 1)]
        gp = [r2(f"gp{s}", [4, P]) for s in range(3)]
        bst = r2("bst", [TT, 6])
        bag = r2("bag", [TT, 2])
        rst = r2("rst", [TT])

        ps = ctx.enter_context(nc.psum_tensor("ps", [P, 8, 512], F32))
        psT = [ps[:, 3 * s:3 * s + 3, 0:GN] for s in (0, 1)]
        g3 = lambda t_: t_.rearrange("p (g n) -> p g n", g=G3)

        w_raw = [S("w_raw0"), S("w_raw1")]
        w_split = S("w_split")
        p_full = S("p_full")
        p_free = [S("p_free0"), S("p_free1")]

        def wsrc(w, rows=0, nrows=D):
            return w[0, rows:rows + nrows, :].rearrange("(k p) n -> p k n", p=P)

        def half(i, per, c):
            return i * (per // 2) + ((c - U_QK) // 2 + 1)


        def load_unit(sp, src, i, per, c):
            sp.wait_ge(w_split, i * per + (c + 1))
            sp.dma_start(wraw[c % 2][:, :, :], src).then_inc(w_raw[c % 2], 16)

        def split_unit(pool, i, per, c, hi, lo):
            raw = wraw[c % 2][:, :, :]
            pool.wait_ge(w_raw[c % 2], i * (8 * per) + 16 * (c // 2 + 1))
            pool.tensor_tensor(hi, raw, ones[:, :].unsqueeze(1).to_broadcast([P, KB, P]), ALU.mult).then_inc(w_hi, 1)
            pool.wait_ge(w_hi, i * per + (c + 1))
            pool.tensor_tensor(lo, raw, hi.bitcast(F32), ALU.subtract).then_inc(w_split, 1)

        w_hi = S("w_hi")

        def split_T(pool, i, per, c):
            pool.wait_ge(p_full, i * per + (c - U_QK + 1))
            split_unit(pool, i, per, c, wh[c % 2][:, :, :], wl[c % 2][:, :, :])

        def unit_T(pe, i, per, c, act_h, act_l, ready=None):
            slot = c % 2
            pe.wait_ge(w_split, i * per + (c + 3))
            pe.wait_ge(p_free[slot], half(i, per, c))
            for k in range(KB):
                if ready is not None:
                    pe.wait_ge(ready[0], ready[1] + k)
                for a, b in ((wh, act_h), (wh, act_l), (wl, act_h)):
                    for g in range(G3):
                        mm = pe.matmul(ps[:, 3 * slot + g, 0:GN], a[slot][:, k, :],
                                       b[:, k, g * GN:(g + 1) * GN],
                                       start=(k == 0 and a is wh and b is act_h),
                                       stop=(k == KB - 1 and a is wl))
                        if k == KB - 1 and a is wl and g == G3 - 1:
                            mm.then_inc(p_full, 1)

        ld_small, ld_tab = S("ld_small"), S("ld_tab")
        ld_x = [S(f"ld_x{t}") for t in range(TT)]
        wm_raw, wm_hi, wm_lo, wm_used = [S(f"wm_raw{s}") for s in range(5)], S("wm_hi"), S("wm_lo"), S("wm_used")
        mod_row, mod_col, cond_hi, ld_diff = S("mod_row"), S("mod_col"), S("cond_hi"), S("ld_diff")
        vec_ps, vec_ok, cond_sig, cond_ok = S("vec_ps"), S("vec_ok"), S("cond_sig"), S("cond_ok")
        init_ok = S("init_ok")
        x_tr, x_cp, x_cpa = S("x_tr"), S("x_cp"), S("x_cpa")
        n1_sq, n1_sqrt, n1_rc, n1_diag, n1_bc, n1_ok = [
            S(f"n1_{k}") for k in ("sq", "sqrt", "rc", "diag", "bc", "ok")]
        mod_ok = S("mod_ok")
        h_t, h_aff, h_hi, h_lo = S("h_t"), S("h_aff"), S("h_hi"), S("h_lo")
        dk = S("dk")
        dka, dkm = S("dka"), S("dkm")
        xT_st = S("xT_st")
        v_full, v_out, v_st = S("v_full"), S("v_out"), [S("v_st0"), S("v_st1")]
        rp_a, rp_mul, rp_out, rp_st = S("rp_a"), S("rp_mul"), S("rp_out"), S("rp_st")
        glu_sig = S("glu_sig")
        gt_sig, gt_st = S("gt_sig"), [S("gt_st0"), S("gt_st1")]
        cv_lat, cv_ctx, cv_sq, cv_ssq, cv_st = S("cv_lat"), S("cv_ctx"), S("cv_sq"), S("cv_ssq"), S("cv_st")
        rope_ld = S("rope_ld")
        w_in_v = wsrc(w_in)
        wmod_v = wsrc(w_mod)
        col = lambda c0, n=P: bass.ds(c0, n)

        with nc.Block() as block:
            @block.sync
            def _(sp):
                rows = [(norm1_g[0], V_N1, 8), (norm2_g[0], V_N2, 8), (conv_b[0], V_CB, 8),
                        (conv_norm_g[0], V_CG, 8), (final_norm_g, V_FG, 8), (c_ctx, V_CC, 8),
                        (c[0], V_C, 8), (b_mod[0], V_BM, 48)]
                for src, r, n in rows:
                    sp.dma_start(vrows[r:r + n, :], src.rearrange("(r p) -> r p", p=P)).then_inc(ld_small, 16)
                sp.dma_start(dwrows[0:CW, :], conv_dw[0]).then_inc(ld_small, 16)
                sp.dma_start(ident[:, :], t_ident).then_inc(ld_small, 16)
                for t in range(TT):
                    src = x_prompt[0] if t == 0 else x_sample[0, (t - 1) * P:t * P, :]
                    sp.dma_start(xnat[:, t, :], src).then_inc(ld_x[t], 16)
                sp.dma_start(coef[:, :, :], t_coef).then_inc(ld_tab, 16)
                sp.dma_start(logit[:, :], ret_decay_logit.rearrange("a b c -> a (b c)").to_broadcast([P, 8])).then_inc(ld_tab, 16)
                for r in range(8):
                    if r >= 3:
                        sp.wait_ge(wm_used, r - 2)
                    sp.dma_start(wmr[r % 3][:, :, :], wmod_v[:, :, r * 256:(r + 1) * 256]).then_inc(wm_raw[r % 3], 16)
                with sp.Fori(0, 2) as i:
                    for j in range(8):
                        load_unit(sp, w_in_v[:, :, col(i * 1024 + (C_V + j * P))], i, 8, j)
                sp.wait_ge(h_lo, KB)
                sp.dma_start(rope[:, :, :], t_rope).then_inc(rope_ld, 16)
                with sp.Fori(0, 8) as i:
                    for j in range(2):
                        load_unit(sp, w_in_v[:, :, col(i * 256 + (C_Q + j * P))], i, 2, U_QK + j)
                sp.wait_ge(v_full, 54)
                with sp.Fori(0, 8) as i:
                    for j in range(2):
                        sp.wait_ge(wm_used, i * 2 + (j + 7))
                        sp.dma_start(wmr[3 + j][:, :, :], wmod_v[:, :, col(i * 512 + (2048 + j * 256), 256)]).then_inc(wm_raw[3 + j], 16)
                        load_unit(sp, w_in_v[:, :, col(i * P + (C_U + j * D))], i, 2, U_U + j)
                with sp.Fori(0, 8) as i:
                    for j in range(4):
                        load_unit(sp, w_in_v[:, :, col(i * 256 + (C_RG + (j // 2) * 2 * D + (j % 2) * P))],
                                  i, 4, U_G + j)

            @block.gpsimd
            def _(pool):
                pool.sem_inc(w_split, 2)
                pool.memset(ones[:, :], 1.0)
                pool.memset(ones_mean[:, :], 1.0 / D)
                pool.memset(epsc[:, :], EPS).then_inc(init_ok, 1)
                pool.wait_ge(init_ok, 1)
                with pool.Fori(0, 2) as i:
                    for s in (0, 1):
                        pool.wait_ge(v_full, i * 18 + 9 * (s + 1))
                        if s == 1:
                            pool.wait_ge(xT_st, 16)
                            pool.wait_ge(h_t, KB)
                        for j in range(4):
                            split_unit(pool, i, 8, 4 * s + j, vsh[s][:, :, j * P:(j + 1) * P],
                                       vsl[s][:, :, j * P:(j + 1) * P])
                with pool.Fori(0, 8) as i:
                    for j in range(2):
                        split_T(pool, i, 2, U_QK + j)
                with pool.Fori(0, 8) as i:
                    for j in range(2):
                        split_T(pool, i, 2, U_U + j)
                pool.wait_ge(h_t, KB)
                pool.memset(ssq[:, :], 0.0).then_inc(cv_ssq, 1)
                with pool.Fori(0, 8) as i:
                    split_T(pool, i, 4, U_G)
                    split_T(pool, i, 4, U_G + 1)
                    pool.wait_ge(cv_ssq, i + 1)
                    pool.wait_ge(cv_sq, i + 1)
                    pool.tensor_tensor(ssq[:, :], ssq[:, :], conv_sq[:, :], ALU.add).then_inc(cv_ssq, 1)
                    split_T(pool, i, 4, U_G + 2)
                    split_T(pool, i, 4, U_G + 3)
                pool.wait_ge(cv_ssq, 9)
                pool.wait_ge(cv_sq, 9)
                pool.tensor_tensor(ssq[:, :], ssq[:, :], conv_sq[:, :], ALU.add).then_inc(cv_ssq, 1)

            @block.scalar
            def _(act):
                act.wait_ge(vec_ok, 2)
                act.activation(small[:, 0:16], vec[:, V_CC:V_CC + 16], ACT.Sigmoid).then_inc(cond_sig, 1)
                for t in range(TT):
                    act.wait_ge(ld_x[t], 16)
                    if t == 0:
                        act.wait_ge(vec_ps, 2)
                        act.wait_ge(vec_ok, 3)
                    else:
                        act.wait_ge(n1_sq, t)
                    act.activation(sqj[:, :], xnat[:, t, :], ACT.Square, scale=1.0 / 32,
                                   accum_out=small[:, 16 + t:17 + t]).then_inc(n1_sq, 1)
                    act.wait_ge(x_tr, 2 * t + 1)
                    act.activation(xT[:, 0:4, t * P:(t + 1) * P],
                                   ps[:, 2 * (t % 3), :].rearrange("p (k n) -> p k n", k=4), ACT.Copy).then_inc(x_cpa, 1)
                act.wait_ge(n1_sq, TT)
                act.wait_ge(init_ok, 1)
                act.activation(small[:, 32:32 + TT], small[:, 16:16 + TT], ACT.Sqrt, bias=epsc[:, :]).then_inc(n1_sqrt, 1)

                def mod_high(slot, turn):
                    act.wait_ge(wm_raw[slot], turn)
                    act.activation(wmh[slot][:, :, :], wmr[slot][:, :, :], ACT.Copy).then_inc(wm_hi, 1)

                mod_high(0, 16)
                mod_high(1, 16)
                act.wait_ge(n1_bc, TT)
                act.activation(g3(ssq[:, :]), psT[0], ACT.Copy).then_inc(n1_ok, 1)
                for r in range(2, 8):
                    mod_high(r % 3, 16 * (r // 3 + 1))
                act.wait_ge(x_cp, TT)
                act.wait_ge(x_cpa, TT)
                act.dma_start(xT_d.rearrange("k p n -> p k n"), xT[:, :, :]).then_inc(xT_st, 16)
                for k in range(KB):
                    act.wait_ge(h_t, k + 1)
                    act.wait_ge(mod_ok, 2)
                    hbk = hb[k % 2]
                    act.activation(hbk[:, 0:P], hbk[:, 0:P], ACT.Identity, scale=scale1[:, k, 0:1],
                                   bias=mod[:, M_SH1 + k, 0:1]).then_inc(h_aff, 1)
                    act.activation(hbk[:, P:T], hbk[:, P:T], ACT.Identity, scale=scale1[:, k, 1:2],
                                   bias=mod[:, M_SH1 + k, 1:2]).then_inc(h_aff, 1)
                    act.wait_ge(h_aff, 2 * k + 2)
                    act.activation(x0h[:, k, :], hbk[:, :], ACT.Copy).then_inc(h_hi, 1)
                act.wait_ge(xT_st, 16)
                act.wait_ge(h_t, KB)
                act.wait_ge(x_tr, 2 * TT)
                act.dma_start(diff0[:, :, :], t_diff).then_inc(ld_diff, 16)
                act.wait_ge(dk, 1)
                act.activation(lgt[:, 1, :], lgt[:, 0, :], ACT.Exp, scale=-1.0).then_inc(dka, 1)
                act.wait_ge(dk, 16)
                for dh in range(8):
                    act.activation(dec[:, dh, :], coef[:, dh // 4, :], ACT.Exp, scale=lgt[:, 7, dh:dh + 1]).then_inc(dka, 1)
                act.wait_ge(ld_diff, 16)
                for h in range(H):
                    if h:
                        act.wait_ge(dk, 17 + 3 * h)
                    for d in (0, 1):
                        act.activation(expd[:, d, :], diff0[:, 2 * d, :], ACT.Exp,
                                       scale=lgt[:, 7, 4 * d + h:4 * d + h + 1]).then_inc(dka, 1)
                with act.Fori(0, 2) as i:
                    for s in (0, 1):
                        for t in range(TT):
                            n = 9 * s + t
                            act.wait_ge(v_out, i * 18 + (n + 7))
                            act.dma_start(v_d[t, :, col(i * 1024 + s * DV, DV)], vout[n % 2][:, :]).then_inc(v_st[n % 2], 16)
                with act.Fori(0, 8) as i:
                    act.wait_ge(p_full, i * 2 + 3)
                    act.wait_ge(rp_out, i * 2 + 2)
                    act.activation(g3(sa[:, :]), psT[0], ACT.Copy).then_inc(p_free[0], 1)
                    for j in (0, 1):
                        act.wait_ge(rp_out, i * 2 + 4)
                        act.dma_start(qk_d[bass.ds(i * 2 + j, 1), :, :].rearrange("a p n -> (a p) n"),
                                      outb[j][:, :]).then_inc(rp_st, 16)
                with act.Fori(0, 8) as i:
                    for j in (0, 1):
                        mod_high(3 + j, i * 16 + 16)
                    act.wait_ge(p_full, i * 2 + (U_U - U_QK + 4))
                    act.wait_ge(p_free[0], half(i, 2, U_U + 0))
                    act.wait_ge(rp_st, 288)
                    act.activation(g3(outb[0][:, :]), psT[1], ACT.Sigmoid).then_inc(p_free[1], 1)
                with act.Fori(0, 8) as i:
                    for j in range(4):
                        act.wait_ge(gt_st[j % 2], i * 32 + 16 * (j // 2 + 1))
                        if j == 0:
                            act.wait_ge(p_free[0], 17)
                        act.wait_ge(p_full, i * 4 + (U_G - U_QK + j + 3))
                        sg = act.activation(g3(outb[j % 2][:, :]), psT[j % 2], ACT.Sigmoid)
                        sg.then_inc(gt_sig, 1) if j < 2 else sg.then_inc(p_free[j % 2], 1)
                        if j < 2:
                            act.wait_ge(p_free[j], half(i, 4, U_G + j) + 1)
                            dst = s_d[bass.ds(i * 2 + j, 1), :, :]
                        else:
                            act.wait_ge(p_free[j % 2], half(i, 4, U_G + j) + 1)
                            dst = b_d[bass.ds(i * 2 + j - 2, 1), :, :]
                        act.dma_start(dst.rearrange("a p n -> (a p) n"), outb[j % 2][:, :]).then_inc(gt_st[j % 2], 16)
                    act.wait_ge(cv_lat, i * CW + CW)
                    act.wait_ge(cv_ctx, i * (CW - 1) + (CW - 1))
                    act.dma_start(conv_d[bass.ds(i, 1), :, :].rearrange("a p n -> (a p) n"),
                                  conv_acc[:, :]).then_inc(cv_st, 16)
                    act.wait_ge(cv_ssq, i + 2)
                    act.activation(conv_sq[:, :], conv_acc[:, :], ACT.Square).then_inc(cv_sq, 1)
                act.wait_ge(cv_st, 144)
                act.wait_ge(xT_st, 16)
                for q in (0, 1):
                    act.wait_ge(v_st[q], 16 + 18 * 16)
                    act.wait_ge(gt_st[q], 16 + 16 * 16)

            @block.vector
            def _(dve):
                dve.sem_inc(p_free[0], 1)
                dve.sem_inc(p_free[1], 1)
                dve.sem_inc(v_out, 6)
                dve.sem_inc(rp_out, 2)
                dve.sem_inc(rp_st, 32)
                dve.sem_inc(cv_st, 16)
                dve.wait_ge(vec_ps, 1)
                dve.tensor_copy(vec[:, :], ps[:, 6, 0:V_ROWS]).then_inc(vec_ok, 1)
                dve.tensor_copy(identr[:, :], ident[:, :]).then_inc(vec_ok, 1)
                dve.wait_ge(vec_ps, 2)
                dve.tensor_copy(convw[:, :, :], ps[:, 7, 0:KB * CW].rearrange("p (k n) -> p k n", k=KB)).then_inc(vec_ok, 1)
                dve.wait_ge(cond_sig, 1)
                dve.tensor_tensor(cond[:, :, 0], vec[:, V_CC:V_CC + 8], small[:, 0:8], ALU.mult)
                dve.tensor_tensor(cond[:, :, 1], vec[:, V_C:V_C + 8], small[:, 8:16], ALU.mult).then_inc(cond_hi, 1)
                dve.wait_ge(cond_hi, 1)
                dve.tensor_copy(condq[:, :, 0:2], cond[:, :, :]).then_inc(cond_hi, 1)
                dve.tensor_tensor(selT[0:4, :], ident[0:4, 0:2], ident[0:4, 2:4], ALU.add)
                dve.wait_ge(cond_hi, 2)
                dve.tensor_tensor(condq[:, :, 2:4], cond[:, :, :], condq[:, :, 0:2].bitcast(F32), ALU.subtract).then_inc(cond_ok, 1)
                for t in range(TT):
                    dve.wait_ge(x_tr, 2 * t + 2)
                    dve.tensor_copy(xT[:, 4:8, t * P:(t + 1) * P],
                                    ps[:, 2 * (t % 3) + 1, :].rearrange("p (k n) -> p k n", k=4)).then_inc(x_cp, 1)
                dve.wait_ge(n1_sqrt, 1)
                dve.reciprocal(small[:, 48:48 + TT], small[:, 32:32 + TT]).then_inc(n1_rc, 1)
                dve.wait_ge(n1_rc, 1)
                for t in range(TT):
                    if t >= 2:
                        dve.wait_ge(n1_bc, t - 1)
                    dve.tensor_scalar(diag[:, t % 2, :], ident[:, :], small[:, 48 + t:49 + t], None, ALU.mult).then_inc(n1_diag, 1)

                def mod_low(slot, turn):
                    dve.wait_ge(wm_hi, turn)
                    dve.tensor_tensor(wml[slot][:, :, :], wmr[slot][:, :, :], wmh[slot][:, :, :].bitcast(F32),
                                      ALU.subtract).then_inc(wm_lo, 1)

                def norm_x(k):
                    dve.tensor_tensor(hb[k % 2][:, :], xT[:, k, :], ssq[:, :], ALU.mult).then_inc(h_t, 1)

                for r in range(9):
                    if r < 8:
                        mod_low(r % 3, r + 1)
                    if r == 0:
                        dve.wait_ge(n1_ok, 1)
                        dve.wait_ge(x_cp, TT)
                        dve.wait_ge(x_cpa, TT)
                        dve.wait_ge(x_tr, 2 * TT)
                        dve.wait_ge(n1_sq, TT)
                    if r in (1, 2):
                        norm_x(r - 1)
                    if r >= 1:
                        dve.wait_ge(wm_used, r)
                        if r >= 3:
                            dve.wait_ge(mod_col, r - 2)
                        dve.tensor_copy(modrow[0:4, (r - 1) % 2, :], ps[0:4, 5 + (r - 1) % 2, 0:256]).then_inc(mod_row, 1)
                dve.wait_ge(mod_col, 8)
                for q in (0, 1):
                    mo = dve.tensor_tensor(mod[:, 0:16, q], ps[:, 7, 0:32].rearrange("p (m q) -> p m q", q=2)[:, :, q],
                                           vec[:, V_BM:V_BM + 16], ALU.add)
                mo.then_inc(mod_ok, 1)
                dve.wait_ge(mod_ok, 1)
                for q in (0, 1):
                    mo = dve.scalar_tensor_tensor(scale1[:, :, q], mod[:, M_SC1:M_SC1 + 8, q], 1.0,
                                                  vec[:, V_N1:V_N1 + 8], ALU.add, ALU.mult)
                mo.then_inc(mod_ok, 1)
                for k in range(KB + 1):
                    if 2 <= k < KB:
                        dve.wait_ge(h_lo, k - 1)
                        norm_x(k)
                    if k >= 1:
                        dve.wait_ge(h_hi, k)
                        dve.tensor_tensor(x0l[:, k - 1, :], hb[(k - 1) % 2][:, :], x0h[:, k - 1, :].bitcast(F32),
                                          ALU.subtract).then_inc(h_lo, 1)
                dve.wait_ge(ld_tab, 32)
                L = lambda r: lgt[:, r, :]
                dve.tensor_scalar(L(1), logit[:, :], -1.0, None, ALU.mult).then_inc(dkm, 1)
                dve.wait_ge(dkm, 1)
                dve.tensor_tensor(L(0), logit[:, :], L(1), ALU.max).then_inc(dk, 1)
                dve.wait_ge(dka, 1)
                dve.tensor_scalar(L(2), L(1), 2.0, None, ALU.add).then_inc(dk, 1)
                dve.wait_ge(dk, 2)
                dve.reciprocal(L(3), L(2)).then_inc(dk, 1)
                dve.wait_ge(dk, 3)
                dve.tensor_tensor(L(4), L(3), L(1), ALU.mult).then_inc(dk, 1)
                dve.wait_ge(dk, 4)
                dve.tensor_tensor(L(5), L(4), L(4), ALU.mult).then_inc(dk, 1)
                dve.wait_ge(dk, 5)
                dve.tensor_scalar(L(6), L(5), 2.0 / 17, 2.0 / 15, ALU.mult, ALU.add).then_inc(dk, 1)
                n = 6
                for q in (13, 11, 9, 7, 5, 3):
                    dve.wait_ge(dk, n)
                    dve.tensor_tensor(L(6), L(6), L(5), ALU.mult).then_inc(dkm, 1)
                    dve.wait_ge(dkm, n - 4)
                    dve.tensor_scalar(L(6), L(6), 2.0 / q, None, ALU.add).then_inc(dk, 1)
                    n += 1
                dve.wait_ge(dk, n)
                dve.tensor_tensor(L(6), L(6), L(5), ALU.mult).then_inc(dk, 1)
                dve.wait_ge(dk, n + 1)
                dve.scalar_tensor_tensor(L(6), L(6), 2.0, L(4), ALU.add, ALU.mult).then_inc(dk, 1)
                dve.tensor_scalar(L(3), logit[:, :], 0.0, None, ALU.min).then_inc(dk, 1)
                dve.wait_ge(dk, n + 3)
                dve.tensor_tensor(L(7), L(3), L(6), ALU.subtract).then_inc(dk, 1)
                assert n + 4 == 16
                dve.wait_ge(dka, 9)
                dve.tensor_scalar(dec[:, :, DKK:DKK + 2], dec[:, :, DKK:DKK + 2], DK ** -0.5, None, ALU.mult).then_inc(dk, 1)
                for h in range(H):
                    dve.wait_ge(dka, 9 + 2 * (h + 1))
                    for d in (0, 1):
                        mk = dve.scalar_tensor_tensor(expd[:, d, :], expd[:, d, :], DK ** -0.5, diff0[:, 2 * d + 1, :],
                                                      ALU.mult, ALU.mult)
                    mk.then_inc(dk, 1)
                    dve.wait_ge(dk, 18 + 3 * h)
                    for jt in (0, 1):
                        x = 128 * (1 - jt)
                        dve.tensor_tensor(masks[:, h, jt, :], expd[:, 0, x:x + 256], expd[:, 1, x:x + 256], ALU.add).then_inc(dk, 1)
                with dve.Fori(0, 2) as i:
                    for s in (0, 1):
                        for t in range(TT):
                            n = 9 * s + t
                            dve.wait_ge(v_full, i * 18 + (n + 19))
                            dve.wait_ge(v_st[n % 2], i * 144 + 16 * (n // 2 + 1))
                            dve.tensor_copy(vout[n % 2][:, :], ps[:, n % 6, :]).then_inc(v_out, 1)
                dve.wait_ge(rope_ld, 16)
                with dve.Fori(0, 8) as i:
                    dve.wait_ge(p_free[0], half(i, 2, U_QK) + 1)
                    dve.wait_ge(rp_st, i * 32 + 32)
                    dve.tensor_tensor(outb[0][:, :], sa[:, :], rope[:, 0, :], ALU.mult)
                    dve.tensor_tensor(outb[1][:, :], sa[:, :], rope[:, 1, :], ALU.mult).then_inc(rp_a, 1)
                    dve.wait_ge(p_full, i * 2 + 4)
                    dve.wait_ge(rp_out, i * 2 + 2)
                    dve.tensor_tensor(g3(rt[:, 0, :]), psT[1], g3(rope[:, 1, :]), ALU.mult).then_inc(rp_mul, 1)
                    dve.tensor_tensor(g3(rt[:, 1, :]), psT[1], g3(rope[:, 0, :]), ALU.mult).then_inc(p_free[1], 1)
                    dve.wait_ge(rp_a, i + 1)
                    dve.wait_ge(rp_mul, i + 1)
                    dve.tensor_tensor(outb[0][:, :], outb[0][:, :], rt[:, 0, :], ALU.subtract).then_inc(rp_out, 1)
                    dve.wait_ge(p_free[1], half(i, 2, U_QK + 1) + 1)
                    dve.tensor_tensor(outb[1][:, :], outb[1][:, :], rt[:, 1, :], ALU.add).then_inc(rp_out, 1)
                with dve.Fori(0, 8) as i:
                    for j in (0, 1):
                        mod_low(3 + j, i * 2 + (9 + j))
                    dve.wait_ge(wm_used, i * 2 + 9)
                    dve.wait_ge(mod_col, i * 2 + 8)
                    dve.tensor_copy(modrow[0:4, 0, :], ps[0:4, 6, 0:256]).then_inc(mod_row, 1)
                    dve.wait_ge(p_free[1], half(i, 2, U_U + 1) + 1)
                    dve.tensor_tensor(g3(glu[:, bass.ds(i, 1), :].rearrange("p a n -> p (a n)")), psT[0],
                                      g3(outb[0][:, :]), ALU.mult).then_inc(p_free[0], 1)
                    dve.wait_ge(wm_used, i * 2 + 10)
                    dve.wait_ge(mod_col, i * 2 + 9)
                    dve.tensor_copy(modrow[0:4, 1, :], ps[0:4, 6, 0:256]).then_inc(mod_row, 1)
                dve.wait_ge(mod_col, 25)
                for q in (0, 1):
                    mo = dve.tensor_tensor(mod[:, 16:48, q], ps[:, 7, 32:96].rearrange("p (m q) -> p m q", q=2)[:, :, q],
                                           vec[:, V_BM + 16:V_BM + 48], ALU.add)
                mo.then_inc(mod_ok, 1)
                dve.wait_ge(mod_ok, 3)
                for q in (0, 1):
                    mo = dve.scalar_tensor_tensor(scale2[:, :, q], mod[:, M_SC2:M_SC2 + 8, q], 1.0,
                                                  vec[:, V_N2:V_N2 + 8], ALU.add, ALU.mult)
                mo.then_inc(mod_ok, 1)
                dve.memset(conv_sq[:, :], 0.0).then_inc(cv_sq, 1)

                def retention_gate(i, j):
                    dve.wait_ge(gt_sig, i * 2 + (j + 1))
                    dve.tensor_tensor(g3(outb[j][:, :]), psT[j], g3(outb[j][:, :]), ALU.mult).then_inc(p_free[j], 1)

                def conv_taps(i, taps):
                    for n in taps:
                        s = n - CW // 2 if n <= CW // 2 - 1 else n - CW // 2 + 1
                        w = convw[:, :, :].rearrange("p k n -> p (k n)")[:, bass.ds(i * CW + (s + CW // 2), 1)]
                        row = glu[:, bass.ds(i, 1), :].rearrange("p a n -> p (a n)")
                        a0, a1 = max(0, -s), max(0, s)
                        for lo_, width, sem, per in ((P, GRID_W, cv_lat, CW), (0, P, cv_ctx, CW - 1)):
                            m = width - abs(s)
                            rows_ = NROW if lo_ else 1
                            dst = conv_acc[:, lo_:lo_ + rows_ * width].rearrange("p (r w) -> p r w", w=width)[:, :, a0:a0 + m]
                            src = row[:, lo_:lo_ + rows_ * width].rearrange("p (r w) -> p r w", w=width)[:, :, a1:a1 + m]
                            if sem is cv_lat:
                                dve.wait_ge(cv_lat, i * CW + (n + 1))
                            elif n == 0:
                                dve.wait_ge(cv_lat, i * CW + 1)
                            else:
                                dve.wait_ge(cv_ctx, i * (CW - 1) + n)
                            dve.scalar_tensor_tensor(dst, src, w, dst, ALU.mult, ALU.add).then_inc(sem, 1)

                with dve.Fori(0, 8) as i:
                    dve.wait_ge(cv_st, i * 16 + 16)
                    dve.wait_ge(cv_sq, i + 1)
                    dve.wait_ge(p_free[0], 17)
                    dve.tensor_scalar(conv_acc[:, :], glu[:, bass.ds(i, 1), :].rearrange("p a n -> p (a n)"),
                                      convw[:, :, :].rearrange("p k n -> p (k n)")[:, bass.ds(i * CW + CW // 2, 1)],
                                      vec[:, bass.ds(i + V_CB, 1)], ALU.mult, ALU.add).then_inc(cv_lat, 1)
                    conv_taps(i, range(0, 9))
                    retention_gate(i, 0)
                    conv_taps(i, range(9, 18))
                    retention_gate(i, 1)
                    conv_taps(i, range(18, 30))

            @block.tensor
            def _(pe):
                pe.sem_inc(p_full, 2)
                pe.sem_inc(v_full, 18)
                for q in (0, 1):
                    pe.sem_inc(v_st[q], 16)
                    pe.sem_inc(gt_st[q], 16)
                pe.wait_ge(ld_small, 160)
                pe.transpose(ps[:, 6, 0:V_ROWS], vrows[0:V_ROWS, :], ident[0:V_ROWS, 0:V_ROWS]).then_inc(vec_ps, 1)
                for k in range(KB):
                    mm = pe.transpose(ps[:, 7, k * CW:(k + 1) * CW], dwrows[0:CW, k * P:(k + 1) * P], ident[0:CW, 0:CW])
                mm.then_inc(vec_ps, 1)
                for t in range(TT):
                    pe.wait_ge(ld_x[t], 16)
                    for b in (0, 1):
                        if t >= 3:
                            pe.wait_ge(x_cpa, t - 2) if b == 0 else pe.wait_ge(x_cp, t - 2)
                        for k in range(4):
                            mm = pe.transpose(ps[:, 2 * (t % 3) + b, k * P:(k + 1) * P],
                                              xnat[:, t, (4 * b + k) * P:(4 * b + k + 1) * P], ident[:, :])
                        mm.then_inc(x_tr, 1)
                pe.wait_ge(init_ok, 1)
                pe.wait_ge(x_cpa, TT)
                pe.wait_ge(x_cp, TT)
                for t in range(TT):
                    pe.wait_ge(n1_diag, t + 1)
                    mm = pe.matmul(ps[:, t // 3, (t % 3) * P:(t % 3 + 1) * P], ones[:, :], diag[:, t % 2, :],
                                   start=True, stop=True)
                    mm.then_inc(n1_bc, 1)

                def mod_rows(slot, bank, turn):
                    pe.wait_ge(wm_lo, turn)
                    for k in range(KB):
                        for w in (wmh, wml):
                            mm = pe.matmul(ps[0:4, bank, 0:256], condq[:, k, :], w[slot][:, k, :],
                                           start=(k == 0 and w is wmh), stop=(k == KB - 1 and w is wml))
                    mm.then_inc(wm_used, 1)

                def mod_cols(s, at_, turn):
                    pe.wait_ge(mod_row, turn)
                    for b in (0, 1):
                        mm = pe.matmul(ps[:, 7, at_ + 2 * b:at_ + 2 * b + 2] if isinstance(at_, int) else
                                       ps[:, 7, bass.ds(at_ + 2 * b, 2)],
                                       modrow[0:4, s, b * P:(b + 1) * P], selT[0:4, :], start=True, stop=True)
                    mm.then_inc(mod_col, 1)

                pe.wait_ge(cond_ok, 1)
                pe.wait_ge(vec_ok, 3)
                for r in range(9):
                    if r < 8:
                        if r >= 2:
                            pe.wait_ge(mod_row, r - 1)
                        mod_rows(r % 3, 5 + r % 2, r + 1)
                    if r >= 1:
                        mod_cols((r - 1) % 2, 4 * (r - 1), r)

                pe.wait_ge(h_lo, KB)
                pe.wait_ge(n1_ok, 1)
                with pe.Fori(0, 2) as i:
                    for s in (0, 1):
                        pe.wait_ge(w_split, i * 8 + (4 * s + 6))
                        for t in range(TT):
                            n = 9 * s + t
                            pe.wait_ge(v_out, i * 18 + (n + 1))
                            for k in range(KB):
                                for a, b in ((x0h, vsh), (x0h, vsl), (x0l, vsh)):
                                    mm = pe.matmul(ps[:, n % 6, :], a[:, k, t * P:(t + 1) * P], b[s][:, k, :],
                                                   start=(k == 0 and a is x0h and b is vsh),
                                                   stop=(k == KB - 1 and a is x0l))
                                    if k == KB - 1 and a is x0l:
                                        mm.then_inc(v_full, 1)
                pe.wait_ge(v_out, 42)
                with pe.Fori(0, 8) as i:
                    for j in range(2):
                        unit_T(pe, i, 2, U_QK + j, x0h, x0l)
                with pe.Fori(0, 8) as i:
                    unit_T(pe, i, 2, U_U, x0h, x0l)
                    mod_cols(1, i * 8 + 28, i * 2 + 8)
                    mod_rows(3, 6, i * 2 + 9)
                    unit_T(pe, i, 2, U_U + 1, x0h, x0l)
                    mod_cols(0, i * 8 + 32, i * 2 + 9)
                    mod_rows(4, 6, i * 2 + 10)
                mod_cols(1, 92, 24)
                with pe.Fori(0, 8) as i:
                    for j in range(4):
                        unit_T(pe, i, 4, U_G + j, x0h, x0l)

        tiles, chunk, norm_tiles, o_pe, o_act, o_dve, o_pool = retention_orders()
        PE_, AC, DV_, PO = Order(o_pe), Order(o_act), Order(o_dve), Order(o_pool)
        pe_done, act_done, dve_done, pool_done = S("pe_done"), S("act_done"), S("dve_done"), S("pool_done")
        q_ld, s0_ld, v_ld, g_ld = [S("q_ld0"), S("q_ld1")], S("s0_ld"), [S(f"v_ld{s}") for s in range(3)], [
            S(f"g_ld{s}") for s in range(3)]
        sp_turn = S("sp_turn")
        g_st, st_st = [S(f"g_st{s}") for s in range(3)], [S("st_st0"), S("st_st1")]
        vorder = [1, 2, 7, 8, 0, 3, 4, 5, 6]
        kv_bank = lambda d, e: 2 + 2 * d + e
        yorder = [s for s in o_pe if s[0] in ("in", "ia")]
        y_bank = lambda *s: 6 + yorder.index(s) % 2
        p_slot = {0: 0, 3: 1, 1: 0, 2: 1, 4: 0}

        def y_reader(*s):
            if s == ("ia", 4, 0):
                return act_done, AC, ("yc",)
            if s[0] == "ia":
                return dve_done, DV_, ("ya", s[1], s[2])
            if s[2] < 2:
                return act_done, AC, ("yt", s[1], s[2], s[3])
            return dve_done, DV_, ("ys", s[1], s[2], s[3])

        with nc.Block() as block:
            @block.sync
            def _(sp):
                with sp.Fori(0, H) as h:
                    hk = lambda p: (h * 2 + (8 - 8 * (p // 2) + p % 2))
                    for p in range(4):
                        prev = [DV_.last(h, "ql", 0), DV_.last(h, "ql", 1), DV_.this(h, "kl", 0), DV_.this(h, "kl", 1)][p]
                        sp.wait_ge(dve_done, prev)
                        sp.dma_start(qst[p % 2][:, :], qk_d[bass.ds(hk(p), 1), :, :].rearrange("a p n -> (a p) n")).then_inc(q_ld[p % 2], 16)
                        if p == 1:
                            for d in (0, 1):
                                sp.wait_ge(st_st[d], h * 16 + 16)
                                sp.wait_ge(pool_done, PO.last(h, "sl", 1, 3, 1))
                                sp.dma_start(sraw[d][:, :, :], state_ret[0, 0, d, bass.ds(h, 1), :, :].rearrange(
                                    "a (k p) n -> p (a k) n", p=P)).then_inc(s0_ld, 16)
                    for x, t in enumerate(vorder):
                        sp.wait_ge(pool_done, PO.last(h, "vl", x + 6) if x < 3 else PO.this(h, "vl", x - 3))
                        if t == 0:
                            sp.sem_inc(sp_turn, 1)
                        sp.dma_start(vst[x % 3][:, :], v_d[t, :, bass.ds(h * DV, DV)]).then_inc(v_ld[x % 3], 16)
                    for x, t in enumerate(norm_tiles):
                        sp.wait_ge(g_st[x % 3], h * 48 + 16 * (x // 3 + 1))
                        if t == 0:
                            sp.sem_inc(sp_turn, 1)
                        sp.dma_start(gp[x % 3][:, :, :], s_d[bass.ds(h * 4, 4), :, t * P:(t + 1) * P].rearrange(
                            "a p n -> p a n")).then_inc(g_ld[x % 3], 16)
                for j in (0, 1):
                    load_unit(sp, wsrc(w_conv_out)[:, :, j * P:(j + 1) * P], 0, 2, U_CONV + j)

            @block.gpsimd
            def _(pool):
                for q in range(3):
                    pool.sem_inc(g_st[q], 16)
                for d in (0, 1):
                    pool.sem_inc(st_st[d], 16)
                pool.sem_inc(pool_done, PO.n)
                with pool.Fori(0, H) as h:
                    PO.pos = 0

                    def v_low(x):
                        pool.wait_ge(act_done, AC.this(h, "vh", x))
                        pool.tensor_tensor(vl[:, vorder[x], :], vst[x % 3][:, :], vh[:, vorder[x], :].bitcast(F32),
                                           ALU.subtract).then_inc(pool_done, PO.one("vl", x))

                    def s_low(d, t, e):
                        pool.wait_ge(act_done, AC.this(h, "sh", d, t, e))
                        pool.tensor_tensor(stl[d][t % 2][:, e, :], sraw[d][:, e, :], sth[d][t % 2][:, e, :].bitcast(F32),
                                           ALU.subtract).then_inc(pool_done, PO.one("sl", d, t, e))

                    for step in o_pool:
                        (v_low if step[0] == "vl" else s_low)(*step[1:])
                for j in (0, 1):
                    split_T(pool, 0, 2, U_CONV + j)

            @block.scalar
            def _(act):
                act.sem_inc(act_done, AC.n)
                with act.Fori(0, H) as h:
                    AC.pos = 0
                    for step in o_act:
                        k, a = step[0], step[1:]
                        if k in ("kh", "qh"):
                            p = a[0]
                            act.wait_ge(q_ld[p], h * 32 + (16 if k == "kh" else 32))
                            act.wait_ge(pe_done, PE_.last(h, "ia", 4, 0))
                            ins = act.activation((kh if k == "kh" else qh)[:, p, :], qst[p][:, :], ACT.Copy)
                        elif k == "vh":
                            x = a[0]
                            act.wait_ge(v_ld[x % 3], h * 48 + 16 * (x // 3 + 1))
                            act.wait_ge(pe_done, PE_.last(h, "ia", 4, 0))
                            ins = act.activation(vh[:, vorder[x], :], vst[x % 3][:, :], ACT.Copy)
                        elif k == "knh":
                            d, t, x = a
                            act.wait_ge(pe_done, PE_.this(h, "kn", d, t))
                            act.wait_ge(dve_done, DV_.this(h, "dec"))
                            if d == 2:
                                act.wait_ge(pe_done, PE_.this(h, "kv", x, 2, 1))
                                ins = act.activation(knh[x][:, 0, :], ps[:, 0, 0:DK], ACT.Copy,
                                                     scale=dech[:, x, DKK + (1 - x):DKK + 2 - x])
                            else:
                                if t:
                                    act.wait_ge(pe_done, PE_.this(h, "kv", d, t - 1, 1))
                                else:
                                    act.wait_ge(pe_done, PE_.last(h, "kv", d, 3, 1))
                                ins = act.activation(knh[d][:, x, :], ps[:, 0, x * DK:(x + 1) * DK], ACT.Copy,
                                                     scale=dech[:, d, DKK + x:DKK + x + 1])
                        elif k == "ph":
                            cc = a[0]
                            act.wait_ge(dve_done, DV_.this(h, "pm", cc))
                            before = {0: PE_.last(h, "ia", 4, 0), 3: PE_.last(h, "ia", 2, 1), 1: PE_.this(h, "ia", 0, 1),
                                      2: PE_.this(h, "ia", 3, 1), 4: PE_.this(h, "ia", 1, 1)}[cc]
                            act.wait_ge(pe_done, before)
                            s = p_slot[cc]
                            ins = act.activation(ph[s][:, 0, 0:P] if cc == 4 else ph[s][:, :, :],
                                                 p32[:, 0, 0:P] if cc == 4 else p32[:, :, :], ACT.Copy)
                        elif k == "sh":
                            d, t, e = a
                            if t == 0:
                                act.wait_ge(s0_ld, h * 32 + 32)
                                act.wait_ge(pe_done, PE_.last(h, "in", d, 2, 1))
                            else:
                                act.wait_ge(dve_done, DV_.this(h, "su", d, t, e))
                                if t >= 2:
                                    act.wait_ge(pe_done, PE_.this(h, "in", d, t - 2, 1))
                                else:
                                    act.wait_ge(pe_done, PE_.last(h, "in", d, 3, 1))
                            ins = act.activation(sth[d][t % 2][:, e, :], sraw[d][:, e, :], ACT.Copy)
                        elif k == "yt":
                            d, t, x = a
                            s = ("in", d, t, x)
                            act.wait_ge(pe_done, PE_.this(h, *s))
                            act.wait_ge(pe_done, PE_.last(h, "tr", TT - 1))
                            ins = act.activation(yb[:, tiles(chunk(d, t))[x], :], ps[:, y_bank(*s), :], ACT.Copy,
                                                 scale=dech[:, d, DQ + x:DQ + x + 1])
                        elif k == "yc":
                            act.wait_ge(pe_done, PE_.this(h, "ia", 4, 0))
                            ins = act.activation(yb[:, 0, :], ps[:, y_bank("ia", 4, 0), :], ACT.Copy)
                        elif k == "so":
                            d, e = a
                            act.wait_ge(pe_done, PE_.this(h, "kv", d, 3, e))
                            act.wait_ge(pool_done, PO.this(h, "sl", d, 3, e))
                            ins = act.activation(sraw[d][:, e, :], ps[:, kv_bank(d, e), :], ACT.Copy)
                        elif k == "sq":
                            n0, n1 = (0, 4) if a[0] == 0 else (4, 9)
                            act.wait_ge(dve_done, DV_.this(h, "ag", n1 - 1))
                            ins = act.activation(rst[:, n0:n1], bag[:, n0:n1, 1], ACT.Sqrt, bias=epsc[:, :])
                        ins.then_inc(act_done, AC.one(*step))
                        if k == "so" and a[1] == 1:
                            act.wait_ge(act_done, AC.this(h, *step))
                            act.dma_start(new_state[0, 0, a[0], bass.ds(h, 1), :, :].rearrange("a (k p) n -> p (a k) n", p=P),
                                          sraw[a[0]][:, :, :]).then_inc(st_st[a[0]], 16)
                    for x, t in enumerate(norm_tiles):
                        act.wait_ge(dve_done, DV_.this(h, "gm", x))
                        act.dma_start(g_d[bass.ds(h * 4, 4), :, t * P:(t + 1) * P].rearrange("a p n -> p a n"),
                                      gp[x % 3][:, :, :]).then_inc(g_st[x % 3], 16)
                for q in range(3):
                    act.wait_ge(g_st[q], 16 + 3 * H * 16)
                for q in (0, 1):
                    act.wait_ge(st_st[q], 16 + H * 16)

            @block.vector
            def _(dve):
                dve.sem_inc(dve_done, DV_.n)
                mrows = masks[:, :, :, :].rearrange("p h a n -> p h (a n)")
                decv = dec[:, :, :].rearrange("p (d h) n -> p h d n", d=2)
                with dve.Fori(0, H) as h:
                    DV_.pos = 0
                    for step in o_dve:
                        k, a = step[0], step[1:]
                        if k == "dec":
                            dve.wait_ge(act_done, AC.last(h, "yt", 1, 1, 1))
                            dve.wait_ge(act_done, AC.last(h, "knh", 2, 0, 1))
                            dve.wait_ge(dve_done, DV_.last(h, "ys", 1, 3, 1))
                            ins = dve.tensor_scalar(dech[:, :, :], decv[:, bass.ds(h, 1), :, :].rearrange("p a d n -> p (a d) n"),
                                                    1.0, None, ALU.mult)
                        elif k == "mask":
                            ins = dve.tensor_scalar(maskh[:, :, :].rearrange("p a n -> p (a n)"),
                                                    mrows[:, bass.ds(h, 1), :].rearrange("p a n -> p (a n)"), 1.0, None, ALU.mult)
                        elif k in ("kl", "ql"):
                            p = a[0]
                            dve.wait_ge(act_done, AC.this(h, k[0] + "h", p))
                            hi, lo = (kh, kl) if k == "kl" else (qh, ql)
                            ins = dve.tensor_tensor(lo[:, p, :], qst[p][:, :], hi[:, p, :].bitcast(F32), ALU.subtract)
                        elif k == "knl":
                            d, t, x = a
                            dve.wait_ge(act_done, AC.this(h, "knh", d, t, 1))
                            if d == 2:
                                ins = dve.scalar_tensor_tensor(knl[x][:, 0, :], ps[:, 0, 0:DK], dech[:, x, DKK + (1 - x):DKK + 2 - x],
                                                               knh[x][:, 0, :].bitcast(F32), ALU.mult, ALU.subtract)
                            else:
                                ins = dve.scalar_tensor_tensor(knl[d][:, x, :], ps[:, 0, x * DK:(x + 1) * DK],
                                                               dech[:, d, DKK + x:DKK + x + 1], knh[d][:, x, :].bitcast(F32),
                                                               ALU.mult, ALU.subtract)
                        elif k == "pm":
                            cc = a[0]
                            dve.wait_ge(pe_done, PE_.this(h, "sc", cc))
                            prev = {0: DV_.last(h, "pl", 4), 3: DV_.this(h, "pl", 0), 1: DV_.this(h, "pl", 3),
                                    2: DV_.this(h, "pl", 1), 4: DV_.this(h, "pl", 2)}[cc]
                            dve.wait_ge(dve_done, prev)
                            dve.wait_ge(dve_done, DV_.this(h, "st", 3) if cc == 4 else DV_.this(h, "mask"))
                            n = P if cc == 4 else 512
                            flat = lambda t_: t_[:, :, :].rearrange("p a n -> p (a n)")[:, 0:n]
                            ins = dve.tensor_tensor(flat(p32), ps[:, 1, 0:n], flat(maskh), ALU.mult)
                        elif k == "pl":
                            cc = a[0]
                            dve.wait_ge(act_done, AC.this(h, "ph", cc))
                            n = P if cc == 4 else 512
                            s = p_slot[cc]
                            flat = lambda t_: t_[:, :, :].rearrange("p a n -> p (a n)")[:, 0:n]
                            ins = dve.tensor_tensor(flat(pl[s]), flat(p32), flat(ph[s]).bitcast(F32), ALU.subtract)
                        elif k == "su":
                            d, t, e = a
                            dve.wait_ge(pe_done, PE_.this(h, "kv", d, t - 1, e))
                            dve.wait_ge(pool_done, PO.this(h, "sl", d, t - 1, e))
                            ins = dve.scalar_tensor_tensor(sraw[d][:, e, :], sraw[d][:, e, :], dech[:, d, DS:DS + 1],
                                                           ps[:, kv_bank(d, e), :], ALU.mult, ALU.add)
                        elif k == "ya":
                            s = ("ia",) + a
                            dve.wait_ge(pe_done, PE_.this(h, *s))
                            t = tiles(a[0])[a[1]]
                            d0, t0 = (0, a[0]) if a[0] < 2 else (1, 3 - a[0])
                            dve.wait_ge(act_done, AC.this(h, "yt", d0, t0, a[1]))
                            ins = dve.tensor_tensor(yb[:, t, :], yb[:, t, :], ps[:, y_bank(*s), :], ALU.add)
                        elif k == "ys":
                            d, t, x = a
                            s = ("in",) + a
                            cc = chunk(d, t)
                            dve.wait_ge(pe_done, PE_.this(h, *s))
                            dve.wait_ge(dve_done, DV_.this(h, "ya", cc, x))
                            ins = dve.scalar_tensor_tensor(yb[:, tiles(cc)[x], :], ps[:, y_bank(*s), :], dech[:, d, DQ + x:DQ + x + 1],
                                                           yb[:, tiles(cc)[x], :], ALU.mult, ALU.add)
                        elif k in ("st", "ag"):
                            n, t = a[0], norm_tiles[a[0]]
                            if k == "ag":
                                ins = dve.bn_aggr(bag[:, n, :], bst[:, n, :])
                            else:
                                if t == 0:
                                    dve.wait_ge(act_done, AC.this(h, "yc"))
                                else:
                                    cc, x = (t - 1) // 2, (t - 1) % 2
                                    dd, t2 = (0, cc) if cc >= 2 else (1, 3 - cc)
                                    dve.wait_ge(dve_done, DV_.this(h, "ys", dd, t2, x))
                                dve.wait_ge(dve_done, DV_.last(h, "yn", n))
                                ins = dve.bn_stats(bst[:, n, :], yb[:, t, :])
                        elif k == "rc":
                            n0, n1 = (0, 4) if a[0] == 0 else (4, 9)
                            dve.wait_ge(act_done, AC.this(h, "sq", a[0]))
                            if a[0] == 0:
                                dve.wait_ge(dve_done, DV_.this(h, "st", 8))
                            ins = dve.reciprocal(rst[:, n0:n1], rst[:, n0:n1])
                        elif k == "yn":
                            n, t = a[0], norm_tiles[a[0]]
                            dve.wait_ge(dve_done, DV_.this(h, "rc", 0 if n < 4 else 1))
                            ins = dve.tensor_scalar(yb[:, t, :], yb[:, t, :], bag[:, n, 0:1], rst[:, n:n + 1],
                                                    ALU.subtract, ALU.mult)
                        elif k == "gm":
                            n = a[0]
                            dve.wait_ge(g_ld[n % 3], h * 48 + 16 * (n // 3 + 1))
                            dve.wait_ge(pe_done, PE_.this(h, "tr", n))
                            ins = dve.tensor_tensor(gp[n % 3][:, :, :], gp[n % 3][:, :, :],
                                                    ps[:, n % 2, :].rearrange("p (a n) -> p a n", a=4), ALU.mult)
                        ins.then_inc(dve_done, DV_.one(*step))

            @block.tensor
            def _(pe):
                pe.sem_inc(pe_done, PE_.n)
                kn_steps = [s for s in o_pe if s[0] == "kn"]
                sc_steps = [s for s in o_pe if s[0] == "sc"]
                with pe.Fori(0, H) as h:
                    PE_.pos = 0

                    def three(out, a, b, first=True, last=True):
                        pe.matmul(out, a[0], b[0], start=first, stop=False)
                        pe.matmul(out, a[0], b[1], start=False, stop=False)
                        return pe.matmul(out, a[1], b[0], start=False, stop=last)

                    for step in o_pe:
                        k, a = step[0], step[1:]
                        if k == "kn":
                            d, t = a
                            if step == kn_steps[0]:
                                pe.wait_ge(dve_done, DV_.this(h, "kl", 1))
                                pe.wait_ge(dve_done, DV_.last(h, "gm", TT - 1))
                            else:
                                before = kn_steps[kn_steps.index(step) - 1]
                                pe.wait_ge(dve_done, DV_.this(h, "knl", before[1], before[2], 1))
                            tl = (0,) if d == 2 else tiles(chunk(d, t))
                            for x, tt in enumerate(tl):
                                for e in (0, 1):
                                    out = ps[:, 0, x * DK + e * P:x * DK + (e + 1) * P]
                                    pe.matmul(out, kh[:, e, tt * P:(tt + 1) * P], identr[:, :], start=True, stop=False)
                                    mm = pe.matmul(out, kl[:, e, tt * P:(tt + 1) * P], identr[:, :], start=False, stop=True)
                        elif k == "sc":
                            cc = a[0]
                            pe.wait_ge(dve_done, DV_.this(h, "ql", 1))
                            if step != sc_steps[0]:
                                pe.wait_ge(dve_done, DV_.this(h, "pm", sc_steps[sc_steps.index(step) - 1][1]))
                            if cc == 4:
                                for e in (0, 1):
                                    mm = three(ps[:, 1, 0:P], (kh[:, e, 0:P], kl[:, e, 0:P]), (qh[:, e, 0:P], ql[:, e, 0:P]),
                                               e == 0, e == 1)
                            else:
                                t0 = tiles(cc)[0]
                                qs = slice(t0 * P, (t0 + 2) * P)
                                for x in (0, 1):
                                    ks = slice((t0 + x) * P, (t0 + x + 1) * P)
                                    for e in (0, 1):
                                        mm = three(ps[:, 1, x * 256:(x + 1) * 256], (kh[:, e, ks], kl[:, e, ks]),
                                                   (qh[:, e, qs], ql[:, e, qs]), e == 0, e == 1)
                        elif k == "kv":
                            d, t, e = a
                            tl = (0,) if t == 3 else tiles(chunk(d, t))
                            if t == 3:
                                pe.wait_ge(dve_done, DV_.this(h, "knl", 2, 0, d))
                                pe.wait_ge(dve_done, DV_.this(h, "su", d, 3, e))
                            else:
                                pe.wait_ge(dve_done, DV_.this(h, "knl", d, t, 1))
                                if t == 0:
                                    pe.wait_ge(act_done, AC.last(h, "so", d, e))
                                else:
                                    pe.wait_ge(dve_done, DV_.this(h, "su", d, t, e))
                            pe.wait_ge(pool_done, PO.this(h, "vl", max(vorder.index(tt) for tt in tl)))
                            for x, tt in enumerate(tl):
                                mm = three(ps[:, kv_bank(d, e), :], [z[d][:, x, e * P:(e + 1) * P] for z in (knh, knl)],
                                           (vh[:, tt, :], vl[:, tt, :]), x == 0, x == len(tl) - 1)
                        elif k in ("in", "ia"):
                            pos = yorder.index(step)
                            if pos >= 2:
                                sem, order, st = y_reader(*yorder[pos - 2])
                                pe.wait_ge(sem, order.this(h, *st))
                            else:
                                last = [s for s in yorder if y_bank(*s) == 6 + pos % 2][-1]
                                sem, order, st = y_reader(*last)
                                pe.wait_ge(sem, order.last(h, *st))
                            out = ps[:, y_bank(*step), :]
                            if k == "in":
                                d, t, x = a
                                pe.wait_ge(pool_done, PO.this(h, "sl", d, t, 1))
                                pe.wait_ge(dve_done, DV_.this(h, "ql", 1))
                                tt = tiles(chunk(d, t))[x]
                                for e in (0, 1):
                                    mm = three(out, [z[:, e, tt * P:(tt + 1) * P] for z in (qh, ql)],
                                               [z[d][t % 2][:, e, :] for z in (sth, stl)], e == 0, e == 1)
                            else:
                                cc, x = a
                                pe.wait_ge(dve_done, DV_.this(h, "pl", cc))
                                s = p_slot[cc]
                                tl = (0,) if cc == 4 else tiles(cc)
                                pe.wait_ge(pool_done, PO.this(h, "vl", max(vorder.index(tt) for tt in tl)))
                                for j, tt in enumerate(tl):
                                    mm = three(out, [z[s][:, j, x * P:(x + 1) * P] for z in (ph, pl)],
                                               (vh[:, tt, :], vl[:, tt, :]), j == 0, j == len(tl) - 1)
                        else:
                            n, t = a[0], norm_tiles[a[0]]
                            pe.wait_ge(dve_done, DV_.this(h, "yn", n))
                            if n >= 2:
                                pe.wait_ge(dve_done, DV_.this(h, "gm", n - 2))
                            elif n == 1:
                                pe.wait_ge(dve_done, DV_.this(h, "pm", 4))
                            else:
                                pe.wait_ge(dve_done, DV_.this(h, "knl", 2, 0, 1))
                            for e in range(4):
                                mm = pe.transpose(ps[:, n % 2, e * P:(e + 1) * P], yb[:, t, e * P:(e + 1) * P], ident[:, :])
                        mm.then_inc(pe_done, PE_.one(*step))

        c_st = at("c_st", [KB, T], X1)
        c_sg = at("c_sg", [2, T], XA)
        ob = at("ob", [TT, D], X0)
        c_ld = [S(f"c_ld{k}") for k in range(KB)]
        rms_ps, rms_sqrt, rms_ok = S("rms_ps"), S("rms_sqrt"), S("rms_ok")
        c_n, c_sig, c_z, c_hi, c_lo = S("c_n"), S("c_sig"), S("c_z"), S("c_hi"), S("c_lo")
        ga_ld, gr_ld, g_hi, g_lo = S("ga_ld"), S("gr_ld"), S("g_hi"), S("g_lo")
        ev = S("ev")
        cb_hi, cb_lo = S("cb_hi"), S("cb_lo")
        sq_ok, sq_add = S("sq_ok"), S("sq_add")
        h2_t, h2_aff, h2_hi, h2_lo = S("h2_t"), S("h2_aff"), S("h2_hi"), S("h2_lo")
        m_sq, m_hi, m_lo = S("m_sq"), S("m_hi"), S("m_lo")
        f_n, o_tr, o_cpa, o_cpd, o_st = S("f_n"), S("o_tr"), S("o_cpa"), S("o_cpd"), S("o_st")
        blk = lambda d_, i: d_[bass.ds(i, 1), :, :].rearrange("a p n -> (a p) n")
        brow = lambda t_, i: t_[:, bass.ds(i, 1), :].rearrange("p a n -> p (a n)")
        parts = lambda slot: [(ps[:, 3 * slot, 0:P], slice(0, P), 0), (ps[:, 3 * slot, P:GN], slice(P, GN), 1),
                              (ps[:, 3 * slot + 1:3 * slot + 3, 0:GN], slice(GN, T), 1)]
        two = lambda t_, sl: t_.rearrange("p (g n) -> p g n", g=2) if sl.start == GN else t_
        branch = [(U_CONV, wsrc(w_conv_out)), (U_RET, wsrc(w_ret_out)), (U_RET + 8, wsrc(w_ret_out, D)), (U_OUT, wsrc(w_out))]
        w2_v = w_mlp2[0].rearrange("(q k p) n -> q p k n", k=KB, p=P)

        with nc.Block() as block:
            @block.sync
            def _(sp):
                for k in range(KB):
                    sp.dma_start(c_st[:, k, :], conv_d[k]).then_inc(c_ld[k], 16)
                for j in range(2, 8):
                    load_unit(sp, branch[0][1][:, :, j * P:(j + 1) * P], 0, 2, U_CONV + j)
                for u0, src in branch[1:]:
                    with sp.Fori(0, 4) as i:
                        for j in range(2):
                            load_unit(sp, src[:, :, col(i * 256 + j * P)], i, 2, u0 + j)
                with sp.Fori(0, 4) as i:
                    for j in range(8):
                        load_unit(sp, wsrc(w_mlp1)[:, :, col(i * D + j * P)], i, 16, U_MLP + j)
                    for j in range(8):
                        load_unit(sp, w2_v[bass.ds(i, 1), :, :, j * P:(j + 1) * P].rearrange("q p k n -> p (q k) n"),
                                  i, 16, U_MLP + 8 + j)
                for t in range(TT):
                    sp.wait_ge(o_cpa, t + 1)
                    sp.wait_ge(o_cpd, t + 1)
                    dst = y_prompt[0] if t == 0 else y_sample[0, (t - 1) * P:t * P, :]
                    sp.dma_start(dst, ob[:, t, :]).then_inc(o_st, 16)
                sp.wait_ge(o_st, 16 * TT)

            @block.gpsimd
            def _(pool):
                for k in range(KB):
                    pool.wait_ge(c_hi, k + 1)
                    pool.tensor_tensor(x0l[:, k, :], c_st[:, k, :], x0h[:, k, :].bitcast(F32), ALU.subtract).then_inc(c_lo, 1)
                for j in range(2, 8):
                    split_T(pool, 0, 2, U_CONV + j)
                for u0, _s in branch[1:]:
                    with pool.Fori(0, 4) as i:
                        for j in range(2):
                            split_T(pool, i, 2, u0 + j)
                with pool.Fori(0, 4) as i:
                    for j in range(16):
                        split_T(pool, i, 16, U_MLP + j)

            def unit_full(i, per, c):
                return i * per + (c - U_QK + 3)

            @block.scalar
            def _(act):
                def root(n):
                    act.wait_ge(rms_ps, n)
                    act.activation(g3(ssq[:, :]), psT[0], ACT.Sqrt, bias=epsc[:, :]).then_inc(rms_sqrt, 1)

                root(1)
                for k in range(KB + 1):
                    if k < KB:
                        act.wait_ge(c_n, k + 1)
                        if k >= 2:
                            act.wait_ge(c_z, k - 1)
                        act.activation(c_sg[:, k % 2, :], c_st[:, k, :], ACT.Sigmoid,
                                       scale=vec[:, V_CG + k:V_CG + k + 1]).then_inc(c_sig, 1)
                    if k >= 1:
                        act.wait_ge(c_z, k)
                        act.activation(x0h[:, k - 1, :], c_st[:, k - 1, :], ACT.Copy).then_inc(c_hi, 1)
                act.wait_ge(c_lo, KB)
                for r, (xh, rows, gates) in enumerate(((x1h, 0, 0), (x0h, 8, 8))):
                    if r == 1:
                        act.wait_ge(p_full, unit_full(0, 2, U_CONV + 7))
                    with act.Fori(0, 4) as i:
                        for j in range(2):
                            act.wait_ge(ev, i * 2 + (8 * r + j + 1))
                            act.dma_start(stage[1][:, :], blk(b_d, i * 2 + (gates + j))).then_inc(ga_ld, 16)
                            act.wait_ge(g_lo, i * 2 + (8 * r + j + 1))
                            act.dma_start(stage[0][:, :], blk(g_d, i * 2 + (rows + j))).then_inc(gr_ld, 16)
                            act.wait_ge(gr_ld, i * 32 + 16 * (8 * r + j + 1))
                            act.activation(brow(xh, i * 2 + j), stage[0][:, :], ACT.Copy).then_inc(g_hi, 1)
                act.wait_ge(p_full, unit_full(0, 2, U_RET + 7))
                with act.Fori(0, 4) as i:
                    for j in range(2):
                        act.wait_ge(ev, i * 2 + (16 + j + 1))
                        act.dma_start(stage[1][:, :], blk(b_d, i * 2 + (8 + j))).then_inc(ga_ld, 16)
                        act.wait_ge(ev, i * 2 + (16 + j + 2))
                        act.activation(brow(x1h, i * 2 + j), brow(acc, i * 2 + j), ACT.Copy).then_inc(cb_hi, 1)
                act.wait_ge(g_lo, 17)
                with act.Fori(0, 4) as i:
                    for j in range(2):
                        act.wait_ge(p_free[1 - j], half(i, 2, U_OUT + j - 1) + 1)
                        act.wait_ge(ev, 25)
                        act.dma_start(stage[1][:, :], blk(xT_d, i * 2 + j)).then_inc(ga_ld, 16)
                        act.wait_ge(p_free[j], half(i, 2, U_OUT + j) + 1)
                        act.wait_ge(sq_add, i * 2 + (j + 1))
                        act.activation(stage[0][:, :], brow(acc, i * 2 + j), ACT.Square).then_inc(sq_ok, 1)
                root(2)
                for k in range(KB):
                    act.wait_ge(h2_t, k + 1)
                    st = stage[k % 2]
                    for q, sl in ((0, slice(0, P)), (1, slice(P, T))):
                        act.activation(st[:, sl], st[:, sl], ACT.Identity, scale=scale2[:, k, q:q + 1],
                                       bias=mod[:, M_SH2 + k, q:q + 1]).then_inc(h2_aff, 1)
                    act.wait_ge(h2_aff, 2 * k + 2)
                    act.activation(x0h[:, k, :], st[:, :], ACT.Copy).then_inc(h2_hi, 1)
                act.wait_ge(h2_lo, KB)
                with act.Fori(0, 4) as i:
                    act.wait_ge(p_full, unit_full(i, 16, U_MLP - 1))
                    for j in range(8):
                        act.wait_ge(p_full, unit_full(i, 16, U_MLP + j))
                        act.wait_ge(m_lo, i * 8 + (j + 1))
                        act.activation(g3(stage[j % 2][:, :]), psT[j % 2], ACT.Relu).then_inc(p_free[j % 2], 1)
                        act.wait_ge(m_sq, i * 8 + (j + 1))
                        act.activation(x1h[:, j, :], stage[j % 2][:, :], ACT.Copy).then_inc(m_hi, 1)
                for k in range(KB):
                    act.wait_ge(p_free[k % 2], half(3, 16, U_MLP + 8 + k) + 1)
                    act.wait_ge(sq_add, 10 + k)
                    act.activation(stage[0][:, :], acc[:, k, :], ACT.Square).then_inc(sq_ok, 1)
                root(3)
                for t in range(TT):
                    act.wait_ge(o_tr, 2 * t + 1)
                    act.activation(ob[:, t, 0:512], ps[:, 2 * (t % 3), :], ACT.Copy).then_inc(o_cpa, 1)

            @block.vector
            def _(dve):
                dve.sem_inc(m_lo, 2)
                dve.sem_inc(ev, 1)
                dve.sem_inc(g_lo, 1)

                def invert(n):
                    dve.wait_ge(rms_sqrt, n)
                    dve.reciprocal(ssq[:, :], ssq[:, :]).then_inc(rms_ok, 1)
                    dve.wait_ge(rms_ok, n)

                invert(1)
                for k in range(KB + 1):
                    if k < KB:
                        dve.wait_ge(c_ld[k], 16)
                        dve.tensor_tensor(c_st[:, k, :], c_st[:, k, :], ssq[:, :], ALU.mult).then_inc(c_n, 1)
                    if k >= 1:
                        dve.wait_ge(c_sig, k)
                        dve.scalar_tensor_tensor(c_st[:, k - 1, :], c_st[:, k - 1, :], vec[:, V_CG + k - 1:V_CG + k],
                                                 c_sg[:, (k - 1) % 2, :], ALU.mult, ALU.mult).then_inc(c_z, 1)
                dve.wait_ge(c_lo, KB)
                for r, xl in enumerate((x1l, x0l, None)):
                    if r == 1:
                        dve.wait_ge(p_full, unit_full(0, 2, U_CONV + 7))
                    with dve.Fori(0, 4) as i:
                        for j in range(2):
                            if r < 2:
                                dve.wait_ge(g_hi, i * 2 + (8 * r + j + 1))
                                xh = (x1h, x0h)[r]
                                dve.tensor_tensor(brow(xl, i * 2 + j), stage[0][:, :], brow(xh, i * 2 + j).bitcast(F32),
                                                  ALU.subtract).then_inc(g_lo, 1)
                            dve.wait_ge(p_full, unit_full(i, 2, U_CONV + 8 * r + j))
                            dve.wait_ge(ga_ld, i * 32 + 16 * (8 * r + j + 1))
                            dve.tensor_tensor(g3(stage[1][:, :]), psT[j], g3(stage[1][:, :]), ALU.mult).then_inc(p_free[j], 1)
                            dve.wait_ge(p_free[j], half(i, 2, U_CONV + 8 * r + j) + 1)
                            if r == 0:
                                dve.tensor_scalar(brow(acc, i * 2 + j), stage[1][:, :], 1.0, None, ALU.mult).then_inc(ev, 1)
                            else:
                                dve.tensor_tensor(brow(acc, i * 2 + j), brow(acc, i * 2 + j), stage[1][:, :], ALU.add).then_inc(ev, 1)
                            if r == 2:
                                dve.wait_ge(cb_hi, i * 2 + (j + 1))
                                dve.tensor_tensor(brow(x1l, i * 2 + j), brow(acc, i * 2 + j), brow(x1h, i * 2 + j).bitcast(F32),
                                                  ALU.subtract).then_inc(cb_lo, 1)
                dve.memset(ssq[:, :], 0.0).then_inc(sq_add, 1)
                with dve.Fori(0, 4) as i:
                    for j in range(2):
                        dve.wait_ge(p_full, unit_full(i, 2, U_OUT + j))
                        dve.wait_ge(ga_ld, i * 32 + 16 * (24 + j + 1))
                        dve.wait_ge(cb_lo, 8)
                        dst = brow(acc, i * 2 + j)
                        for src, sl, q in parts(j):
                            gate = mod[:, bass.ds(i * 2 + (M_G1 + j), 1), q:q + 1].rearrange("p a b -> p (a b)")
                            x = dve.scalar_tensor_tensor(two(dst[:, sl], sl), src, gate, two(stage[1][:, sl], sl), ALU.mult, ALU.add)
                        x.then_inc(p_free[j], 1)
                        dve.wait_ge(sq_ok, i * 2 + (j + 1))
                        dve.tensor_tensor(ssq[:, :], ssq[:, :], stage[0][:, :], ALU.add).then_inc(sq_add, 1)
                invert(2)
                for k in range(KB + 1):
                    if k < KB:
                        if k >= 2:
                            dve.wait_ge(h2_lo, k - 1)
                        dve.tensor_tensor(stage[k % 2][:, :], acc[:, k, :], ssq[:, :], ALU.mult).then_inc(h2_t, 1)
                    if k >= 1:
                        dve.wait_ge(h2_hi, k)
                        dve.tensor_tensor(x0l[:, k - 1, :], stage[(k - 1) % 2][:, :], x0h[:, k - 1, :].bitcast(F32),
                                          ALU.subtract).then_inc(h2_lo, 1)
                dve.memset(ssq[:, :], 0.0).then_inc(sq_add, 1)
                with dve.Fori(0, 4) as i:
                    for j in range(8):
                        dve.wait_ge(p_free[j % 2], half(i, 16, U_MLP + j) + 1)
                        dve.tensor_tensor(stage[j % 2][:, :], stage[j % 2][:, :], stage[j % 2][:, :], ALU.mult).then_inc(m_sq, 1)
                        dve.wait_ge(m_hi, i * 8 + (j + 1))
                        dve.tensor_tensor(x1l[:, j, :], stage[j % 2][:, :], x1h[:, j, :].bitcast(F32), ALU.subtract).then_inc(m_lo, 1)
                    for j in range(8):
                        dve.wait_ge(p_full, unit_full(i, 16, U_MLP + 8 + j))
                        if j < 2:
                            dve.wait_ge(p_free[j], half(i, 16, U_MLP + j))
                        dst = acc[:, j, :]
                        for src, sl, q in parts(j % 2):
                            x = dve.scalar_tensor_tensor(two(dst[:, sl], sl), src, mod[:, M_G2 + j, q:q + 1],
                                                         two(dst[:, sl], sl), ALU.mult, ALU.add)
                        x.then_inc(p_free[j % 2], 1)
                for k in range(KB):
                    dve.wait_ge(sq_ok, 9 + k)
                    dve.tensor_tensor(ssq[:, :], ssq[:, :], stage[0][:, :], ALU.add).then_inc(sq_add, 1)
                invert(3)
                for k in range(KB):
                    dve.scalar_tensor_tensor(acc[:, k, :], acc[:, k, :], vec[:, V_FG + k:V_FG + k + 1], ssq[:, :],
                                             ALU.mult, ALU.mult).then_inc(f_n, 1)
                for t in range(TT):
                    dve.wait_ge(o_tr, 2 * t + 2)
                    dve.tensor_copy(ob[:, t, 512:D], ps[:, 2 * (t % 3) + 1, :]).then_inc(o_cpd, 1)

            @block.tensor
            def _(pe):
                def mean_square():
                    for g in range(G3):
                        mm = pe.matmul(ps[:, g, 0:GN], ones_mean[:, :], ssq[:, g * GN:(g + 1) * GN], start=True, stop=True)
                    mm.then_inc(rms_ps, 1)

                mean_square()
                for u0, ready, xh, xl in ((U_CONV, (c_lo, 1), x0h, x0l), (U_RET, (g_lo, 2), x1h, x1l),
                                          (U_RET + 8, (g_lo, 10), x0h, x0l), (U_OUT, (cb_lo, 1), x1h, x1l)):
                    with pe.Fori(0, 4) as i:
                        for j in range(2):
                            unit_T(pe, i, 2, u0 + j, xh, xl, ready)
                pe.wait_ge(sq_add, 9)
                pe.wait_ge(p_free[0], half(0, 16, U_MLP))
                mean_square()
                pe.wait_ge(h2_t, 1)
                with pe.Fori(0, 4) as i:
                    for j in range(8):
                        unit_T(pe, i, 16, U_MLP + j, x0h, x0l, (h2_lo, 1))
                    for j in range(8):
                        unit_T(pe, i, 16, U_MLP + 8 + j, x1h, x1l, (m_lo, i * 8 + 3))
                pe.wait_ge(sq_add, 18)
                mean_square()
                pe.wait_ge(f_n, KB)
                for t in range(TT):
                    for b in (0, 1):
                        if t >= 3:
                            pe.wait_ge(o_cpa, t - 2) if b == 0 else pe.wait_ge(o_cpd, t - 2)
                        for k in range(4):
                            mm = pe.transpose(ps[:, 2 * (t % 3) + b, k * P:(k + 1) * P],
                                              acc[:, 4 * b + k, t * P:(t + 1) * P], ident[:, :])
                        mm.then_inc(o_tr, 1)


def shape_tables():
    p, x = np.arange(P, dtype=np.float32)[:, None], np.arange(GN, dtype=np.float32)[None, :]
    nf = DK // 4
    inv = np.float32(10000.0) ** (-np.arange(nf, dtype=np.float32) / np.float32(nf))
    tok = np.arange(T - P)
    ang = np.concatenate([(tok // GRID_W).astype(np.float32)[:, None] * inv,
                          (tok % GRID_W).astype(np.float32)[:, None] * inv], axis=-1).astype(np.float32)
    rope = np.zeros((P, 2, T), np.float32)
    rope[:, 0, :P] = 1.0
    rope[:, 0, P:] = np.cos(ang).T
    rope[:, 1, P:] = np.sin(ang).T
    c = 2 * P
    coef = np.stack([np.concatenate([p + 1, p + P + 1, c - 1 - p, P - 1 - p, 0 * p + c], 1),
                     np.concatenate([c - p, P - p, p, p + P, 0 * p + c], 1)], 1)
    d = (x - P) - p
    diff = np.stack([np.maximum(d, 0), d >= 0, np.maximum(-d, 0), d <= 0], 1)
    return {"ident": np.eye(P, dtype=np.float32), "rope": rope, "coef": coef.astype(np.float32),
            "diff": diff.astype(np.float32)}


_INS = ["x_prompt", "x_sample", "c", "state_ret", "c_ctx", "norm1_g", "norm2_g", "w_mod", "b_mod", "w_in",
        "conv_dw", "conv_b", "conv_norm_g", "w_conv_out", "ret_decay_logit", "w_ret_out", "w_out",
        "w_mlp1", "w_mlp2", "final_norm_g"]
_OUTS = [(1, 128, 1024), (1, 1024, 1024), (1, 1, 2, 4, 256, 512)]


def kernel(**inputs):
    import concourse.bacc as _bacc
    from concourse.bass_utils import run_bass_kernel_spmd as _run

    nc = _bacc.Bacc("TRN2", target_bir_lowering=False, num_devices=1, dynamic_dma_scratch_size=1024)
    arrays, args = {}, []
    given = {**{n: inputs[n] for n in _INS}, **shape_tables()}
    for name, a in given.items():
        arrays[f"in_{name}"] = np.ascontiguousarray(a)
        args.append(nc.dram_tensor(f"in_{name}", a.shape, F32, kind="ExternalInput").ap())
    for i, shape in enumerate(_OUTS):
        args.append(nc.dram_tensor(f"out_{i}", shape, F32, kind="ExternalOutput").ap())
    step_kernel(nc, *args)
    r = _run(nc, [arrays], core_ids=[0])
    return tuple(r.results[0][f"out_{i}"] for i in range(len(_OUTS)))
```

```python
from contextlib import ExitStack

import numpy as np
import concourse.bass as bass
from concourse import mybir

F32 = mybir.dt.float32
F32R = mybir.dt.float32r
ALU = mybir.AluOpType
ACT = mybir.ActivationFunctionType

P = 128
D = 1024
KB = D // P
T = 1152
TT = T // P
G3, GN = 3, 384
H, DK, DV = 4, 256, 512
CW = 31
GRID_W = 64
NROW = 1024 // GRID_W
MLP = 4096
V_WITH = (2, 3, 6, 7)
GP = 7
EPS = 1e-6
BLK = T * 4

U_V, U_QK, U_U, U_G, U_CONV, U_RET, U_OUT, U_MLP = 0, 16, 32, 48, 80, 88, 104, 112
C_U, C_Q, C_V, C_RG = 0, 2 * D, 2 * D + 2 * H * DK, 2 * D + 2 * H * DK + H * DV
V_N1, V_N2, V_CB, V_CG, V_FG, V_CC, V_C, V_BM, V_ROWS = 0, 8, 16, 24, 32, 40, 48, 56, 104
M_SH1, M_SC1, M_G1, M_SH2, M_SC2, M_G2 = 0, 8, 16, 24, 32, 40
DQ, DKK, DS = 0, 2, 4


def late(step):
    k, a = step[0], step[1:]
    if k in ("in", "ys"):
        return a[1] >= 2
    if k in ("kv", "su", "sh", "sl"):
        return a[1] == 3
    if k in ("kn", "knh", "knl"):
        return a[0] == 2
    if k in ("sc", "ia", "pm", "ph", "pl"):
        return a[0] == 4
    return k in ("tr", "so", "yc", "sq", "dcl", "st", "sep", "ag", "rc", "nm", "yn", "yna", "gm", "gs")


def retention_orders():
    tiles = lambda c: (1 + 2 * c, 2 + 2 * c)
    chunk = lambda d, t: t if d == 0 else 3 - t
    norm_tiles = [3, 4, 5, 6, 1, 2, 7, 8, 0]
    two = lambda *s: [s + (x,) for x in (0, 1)]
    some = lambda k, *xs: [(k, x) for x in xs]

    pe = [("kn", 2, 0), ("sc", 4)] + two("in", 0, 2) + two("in", 1, 2) + two("in", 0, 3) + two("kv", 0, 3)
    pe += two("in", 1, 3) + [("kn", 0, 0)] + two("kv", 1, 3) + [("ia", 4, 0), ("kn", 1, 0)]
    pe += two("kv", 0, 0) + two("kv", 1, 0) + [("sc", 0)]
    pe += some("tr", 0, 1) + [("kn", 0, 1)] + some("tr", 2, 3, 4) + [("sc", 3)] + some("tr", 5, 6) + [("kn", 1, 1)]
    pe += some("tr", 7, 8) + two("in", 0, 0) + two("ia", 0) + two("in", 1, 0) + two("ia", 3)
    pe += [("sc", 1)] + two("kv", 0, 1) + two("kv", 1, 1) + [("kn", 0, 2), ("sc", 2)] + two("in", 0, 1)
    pe += [("kn", 1, 2)] + two("ia", 1) + two("in", 1, 1) + two("ia", 2) + two("kv", 0, 2) + two("kv", 1, 2)

    act = two("knh", 2, 0) + two("sh", 0, 3) + [("ph", 4)] + two("sh", 1, 3) + some("kh", 0, 1)
    act += some("vh", 0, 1) + two("so", 0) + two("knh", 0, 0) + some("vh", 2, 3) + two("so", 1)
    act += some("qh", 0) + two("knh", 1, 0) + some("qh", 1) + [("yc",)] + [("sq",)] + two("sh", 0, 0) + some("yna", 1)
    act += two("sh", 1, 0) + some("gs", 0) + some("yna", 3) + [("ph", 0)] + two("knh", 0, 1) + some("yna", 5, 7) + some("gs", 1)
    act += some("vh", 4, 5) + some("gs", 2) + two("sh", 0, 1) + some("gs", 3, 4) + some("vh", 6, 7)
    act += two("knh", 1, 1) + [("ph", 3)] + two("yt", 0, 0) + two("sh", 1, 1)
    act += some("gs", 5, 6, 7, 8) + [("vh", 8)] + two("yt", 1, 0)
    act += [("ph", 1)] + two("sh", 0, 2) + two("sh", 1, 2) + two("knh", 0, 2)
    act += [("ph", 2)] + two("yt", 0, 1) + two("knh", 1, 2) + two("yt", 1, 1)

    dve = [("dcl",)] + two("su", 0, 3) + two("knl", 2, 0) + [("ys", 0, 2, 0)] + two("su", 1, 3)
    dve += [("ys", 0, 2, 1), ("pm", 4)] + two("ys", 1, 2) + [("pl", 4), ("dec",)] + some("kl", 0, 1)
    dve += two("ys", 0, 3) + some("st", 0, 1) + two("ys", 1, 3) + two("knl", 0, 0)
    dve += some("st", 2, 3, 4, 5) + two("knl", 1, 0) + some("st", 6, 7, 8) + [("sep",), ("mask",)]
    dve += some("ag", *range(9)) + [("rc",), ("nm",)]
    dve += some("yn", 0, 2) + some("gm", 0) + some("yn", 4) + some("gm", 1) + [("pm", 0)] + some("gm", 2)
    dve += some("yn", 6) + two("knl", 0, 1) + some("gm", 3) + [("su", 0, 1, 0)] + some("gm", 4) + [("su", 0, 1, 1)]
    dve += some("yn", 8) + some("gm", 5) + [("pl", 0)] + some("gm", 6, 7) + [("pm", 3)] + some("gm", 8)
    dve += two("knl", 1, 1) + two("su", 1, 1) + [("pl", 3)]
    dve += two("ya", 0) + two("ya", 3)
    dve += [("pm", 1), ("pl", 1)] + two("su", 0, 2) + two("su", 1, 2)
    dve += two("knl", 0, 2) + [("pm", 2), ("pl", 2)] + two("knl", 1, 2) + two("ya", 1) + two("ya", 2)

    pool = two("sl", 0, 3) + two("sl", 1, 3) + some("vl", 0, 1, 2, 3) + some("ql", 0, 1) + two("sl", 0, 0) + two("sl", 1, 0)
    pool += some("vl", 4, 5) + two("sl", 0, 1) + some("vl", 6, 7) + two("sl", 1, 1) + some("vl", 8)
    pool += two("sl", 0, 2) + two("sl", 1, 2)
    return tiles, chunk, norm_tiles, pe, act, dve, pool


class At:

    def __init__(self, i, phase):
        self.i, self.phase, self.late = i, phase, 0

    def has(self, step):
        return not (self.phase == "first" and late(step) or self.phase == "last" and not late(step))

    def head(self, per, add):
        return self.i * per + (add - per * self.late)


class Order:

    def __init__(self, steps):
        self.steps = [s for s in steps if s[0] != "gs"]
        self.n = len(self.steps)
        self.at = {s: k for k, s in enumerate(self.steps)}
        assert len(self.at) == self.n
        self.start = [late(s) for s in self.steps].index(False)

    def this(self, at, *step, back=0):
        rel = late(step) - at.late - back
        assert rel in (0, -1), step
        if (rel == 0 and not at.has(step)) or (rel == -1 and at.phase == "first"):
            return None
        return self.count(at, rel, step)

    def count(self, at, rel, step):
        place = rel * self.n + self.at[step] + 1
        return place, at.i * self.n + place

    def last(self, at, *step):
        return self.this(at, *step, back=1)

    def one(self, at, *step):
        k = m = self.at[step]
        while m + 1 < self.n and not at.has(self.steps[m + 1]):
            m += 1
        return m - k + 1


def step_kernel(nc, x_prompt, x_sample, c, state_ret, c_ctx, norm1_g, norm2_g, w_mod, b_mod, w_in,
                conv_dw, conv_b, conv_norm_g, w_conv_out, ret_decay_logit, w_ret_out, w_out,
                w_mlp1, w_mlp2, final_norm_g, t_ident, t_rope, t_coef, t_diff,
                y_prompt, y_sample, new_state):
    ctx = ExitStack()
    with ctx:
        S = lambda name: ctx.enter_context(nc.semaphore(name))
        dram = lambda name, shape: nc.dram_tensor(name, shape, F32, kind="Internal").ap()
        xT_d, conv_d = dram("xT_d", [KB, P, T]), dram("conv_d", [KB, P, T])
        qk_d, v_d = dram("qk_d", [16, P, T]), dram("v_d", [TT, P, H * DV])
        s_d, b_d, g_d = dram("s_d", [16, P, T]), dram("b_d", [16, P, T]), dram("g_d", [16, P, T])

        top = [(nc.sbuf_base + 31) // 32 * 32]

        def at(name, shape, off, dt=F32):
            return nc.alloc_sbuf_tensor_at(name, [P] + shape, dt, offset=off)

        def room(nbytes):
            off = top[0]
            top[0] += (nbytes + 31) // 32 * 32
            assert top[0] <= nc.sbuf_usable_end, (top[0], nc.sbuf_usable_end)
            return off

        ident = at("ident", [P], room(512))
        identr = at("identr", [P], room(512), F32R)
        ones = at("ones", [P], room(512))
        ones_mean = at("ones_mean", [P], room(512))
        vec = at("vec", [V_ROWS], room(416))
        cond = at("cond", [KB, 2], room(64))
        mod = at("mod", [48, 2], room(384))
        scale1 = at("scale1", [KB, 2], room(64))
        scale2 = at("scale2", [KB, 2], room(64))
        dec = at("dec", [8, 5], room(160))
        dech = at("dech", [2, 5], room(64))
        convw = at("convw", [KB, CW], room(992))
        epsc = at("epsc", [1], room(32))
        SMALL = room(256)
        small = at("small", [64], SMALL)
        ssq = at("ssq", [T], room(BLK))
        wraw = [at(f"wraw{s}", [KB, P], room(4096)) for s in (0, 1)]
        wh = [at(f"wh{s}", [KB, P], room(4096), F32R) for s in (0, 1)]
        wl = [at(f"wl{s}", [KB, P], room(4096), F32R) for s in (0, 1)]
        X0, X1, XA = room(16 * BLK), room(16 * BLK), room(8 * BLK)
        XS = room(2 * BLK)
        XEND = nc.sbuf_usable_end
        x0h, x0l = at("x0h", [KB, T], X0, F32R), at("x0l", [KB, T], X0 + 8 * BLK, F32R)
        x1h, x1l = at("x1h", [KB, T], X1, F32R), at("x1l", [KB, T], X1 + 8 * BLK, F32R)
        acc = at("acc", [KB, T], XA)
        stage = [at(f"stage{s}", [T], XS + s * BLK) for s in (0, 1)]

        B1 = X1
        vsh = [at("vs0h", [KB, 512], B1, F32R), at("vs1h", [KB, 512], B1 + 32768, F32R)]
        vsl = [at("vs0l", [KB, 512], B1 + 16384, F32R), at("vs1l", [KB, 512], B1 + 32768 + 16384, F32R)]
        wm_at = [X0 + 20480, X0 + 36864, X0 + 53248, B1, B1 + 16384]
        wmr = [at(f"wmr{s}", [KB, 256], a) for s, a in enumerate(wm_at)]
        wml = [at(f"wml{s}", [KB, 256], a, F32R) for s, a in enumerate(wm_at)]
        wmh = [at(f"wmh{s}", [KB, 256], a + 8192, F32R) for s, a in enumerate(wm_at)]
        xT = at("xT", [KB, T], B1 + 32768)
        glu = at("glu", [KB, T], B1 + 32768)
        XM = B1 + 32768 + 8 * BLK
        xnat = at("xnat", [TT, D], XM)
        rope = at("rope", [2, T], XM)
        conv_acc = at("conv_acc", [T], XM)
        conv_sq = at("conv_sq", [T], XM + BLK)
        vout = [at(f"vout{s}", [DV], XM + 2 * BLK + 2048 * s) for s in (0, 1)]
        outb = [at(f"outb{s}", [T], XM + 2 * BLK + 4096 + BLK * s) for s in (0, 1)]
        rt = at("rt", [2, T], XM + 4 * BLK + 4096)
        sa = at("sa", [T], XM + 6 * BLK + 4096)
        XK = XM + 8 * BLK
        masks = at("masks", [H, 2, 256], XK)
        XE = XK + 8192
        vrows = at("vrows", [P], XE)
        dwrows = at("dwrows", [D], X0)
        coef = at("coef", [2, 5], XE + 512)
        logit = at("logit", [8], XE + 576)
        lgt = at("lgt", [8, 8], XE + 608)
        expd = at("expd", [2, GN], B1 + 65536)
        diff0 = at("diff0", [4, GN], XM + 28672)
        assert XM + 6 * BLK + 4096 + BLK <= XM + 8 * BLK
        sqj = at("sqj", [D], X0 + 16384)
        diag = at("diag", [2, P], XE + 864)
        hb = [at(f"hb{s}", [T], XM + BLK * s) for s in (0, 1)]
        condq = at("condq", [KB, 4], XE + 1888, F32R)
        selT = at("selT", [2], XE + 2016)
        modrow = at("modrow", [2, 256], XE + 2048)
        assert XE + 2048 + 2048 <= XEND, (XE + 4096 - XEND)

        o = [X0]

        def r2(name, shape, dt=F32, n=1):
            size = (4 * int(np.prod(shape)) + 31) // 32 * 32
            if o[0] < XE and o[0] + size > XK:
                o[0] = XE
            t_ = at(name, shape, o[0], dt)
            o[0] += size
            assert o[0] <= XEND, (name, o[0], XEND)
            return t_

        kh, kl = r2("kh", [2, T], F32R), r2("kl", [2, T], F32R)
        qh, ql = r2("qh", [2, T], F32R), r2("ql", [2, T], F32R)
        vh, vl = r2("vh", [TT, DV], F32R), r2("vl", [TT, DV], F32R)
        sth = [[r2(f"sth{d}{s}", [2, DV], F32R) for s in (0, 1)] for d in (0, 1)]
        stl = [[r2(f"stl{d}{s}", [2, DV], F32R) for s in (0, 1)] for d in (0, 1)]
        sraw = [r2(f"sraw{d}", [2, DV]) for d in (0, 1)]
        knh = [r2(f"knh{d}", [2, DK], F32R) for d in (0, 1)]
        knl = [r2(f"knl{d}", [2, DK], F32R) for d in (0, 1)]
        p32 = r2("p32", [2, 256])
        ph = [r2(f"ph{s}", [2, 256], F32R) for s in (0, 1)]
        pl = [r2(f"pl{s}", [2, 256], F32R) for s in (0, 1)]
        yb = r2("yb", [TT, DV])
        maskh = r2("maskh", [2, 256])
        dechl = r2("dechl", [2, 5])
        vst = [r2(f"vst{s}", [DV]) for s in range(3)]
        qst = [r2(f"qst{s}", [T]) for s in (0, 1)]
        gp = [r2(f"gp{s}", [4, P]) for s in range(GP)]
        bst = r2("bst", [TT, 6])
        bag = r2("bag", [TT, 2])
        rst = at("rst", [TT], SMALL)
        nmr = at("nmr", [TT], SMALL + 64)

        ps = ctx.enter_context(nc.psum_tensor("ps", [P, 8, 512], F32))
        psT = [ps[:, 3 * s:3 * s + 3, 0:GN] for s in (0, 1)]
        g3 = lambda t_: t_.rearrange("p (g n) -> p g n", g=G3)

        w_raw = [S("w_raw0"), S("w_raw1")]
        w_split = S("w_split")
        p_full = S("p_full")
        p_free = [S("p_free0"), S("p_free1")]

        def wsrc(w, rows=0, nrows=D):
            return w[0, rows:rows + nrows, :].rearrange("(k p) n -> p k n", p=P)

        def half(i, per, c):
            return i * (per // 2) + ((c - U_QK) // 2 + 1)


        def load_unit(sp, src, i, per, c):
            sp.wait_ge(w_split, i * per + (c + 1))
            sp.dma_start(wraw[c % 2][:, :, :], src).then_inc(w_raw[c % 2], 16)

        def split_unit(pool, i, per, c, hi, lo):
            raw = wraw[c % 2][:, :, :]
            pool.wait_ge(w_raw[c % 2], i * (8 * per) + 16 * (c // 2 + 1))
            pool.tensor_tensor(hi, raw, ones[:, :].unsqueeze(1).to_broadcast([P, KB, P]), ALU.mult).then_inc(w_hi, 1)
            pool.wait_ge(w_hi, i * per + (c + 1))
            pool.tensor_tensor(lo, raw, hi.bitcast(F32), ALU.subtract).then_inc(w_split, 1)

        w_hi = S("w_hi")

        def split_T(pool, i, per, c):
            pool.wait_ge(p_full, i * per + (c - U_QK + 1))
            split_unit(pool, i, per, c, wh[c % 2][:, :, :], wl[c % 2][:, :, :])

        def unit_T(pe, i, per, c, act_h, act_l, ready=None, pair=False):
            units = (c, c + 1) if pair else (c,)
            for k in range(KB):
                if ready is not None:
                    pe.wait_ge(ready[0], ready[1] + k)
                for u in units:
                    slot = u % 2
                    if k == 0:
                        pe.wait_ge(w_split, i * per + (u + 3))
                        pe.wait_ge(p_free[slot], half(i, per, u))
                    for a, b in ((wh, act_h), (wh, act_l), (wl, act_h)):
                        for g in range(G3):
                            mm = pe.matmul(ps[:, 3 * slot + g, 0:GN], a[slot][:, k, :],
                                           b[:, k, g * GN:(g + 1) * GN],
                                           start=(k == 0 and a is wh and b is act_h),
                                           stop=(k == KB - 1 and a is wl))
                            if k == KB - 1 and a is wl and g == G3 - 1:
                                mm.then_inc(p_full, 1)

        ld_small, ld_tab = S("ld_small"), S("ld_tab")
        ld_x = [S(f"ld_x{t}") for t in range(TT)]
        wm_raw, wm_hi, wm_lo, wm_used = [S(f"wm_raw{s}") for s in range(5)], S("wm_hi"), S("wm_lo"), S("wm_used")
        mod_row, mod_col, cond_hi, ld_diff = S("mod_row"), S("mod_col"), S("cond_hi"), S("ld_diff")
        vec_ps, vec_ok, cond_sig, cond_ok = S("vec_ps"), S("vec_ok"), S("cond_sig"), S("cond_ok")
        init_ok = S("init_ok")
        x_tr, x_cp, x_cpa = S("x_tr"), S("x_cp"), S("x_cpa")
        n1_sq, n1_sqrt, n1_rc, n1_diag, n1_bc, n1_ok = [
            S(f"n1_{k}") for k in ("sq", "sqrt", "rc", "diag", "bc", "ok")]
        mod_ok = S("mod_ok")
        h_t, h_aff, h_hi, h_lo = S("h_t"), S("h_aff"), S("h_hi"), S("h_lo")
        dk = S("dk")
        dka, dkm = S("dka"), S("dkm")
        xT_st = S("xT_st")
        v_full, v_out, v_st = S("v_full"), S("v_out"), [S("v_st0"), S("v_st1")]
        rp_a, rp_mul, rp_out, rp_st = S("rp_a"), S("rp_mul"), S("rp_out"), S("rp_st")
        glu_ok = S("glu_ok")
        gt_sig, gt_st = S("gt_sig"), [S("gt_st0"), S("gt_st1")]
        cv_lat, cv_ctx, cv_sq, cv_ssq, cv_st = S("cv_lat"), S("cv_ctx"), S("cv_sq"), S("cv_ssq"), S("cv_st")
        rope_ld = S("rope_ld")
        w_in_v = wsrc(w_in)
        wmod_v = wsrc(w_mod)
        col = lambda c0, n=P: bass.ds(c0, n)

        with nc.Block() as block:
            @block.sync
            def _(sp):
                rows = [(norm1_g[0], V_N1, 8), (norm2_g[0], V_N2, 8), (conv_b[0], V_CB, 8),
                        (conv_norm_g[0], V_CG, 8), (final_norm_g, V_FG, 8), (c_ctx, V_CC, 8),
                        (c[0], V_C, 8), (b_mod[0], V_BM, 48)]
                for src, r, n in rows:
                    sp.dma_start(vrows[r:r + n, :], src.rearrange("(r p) -> r p", p=P)).then_inc(ld_small, 16)
                sp.dma_start(dwrows[0:CW, :], conv_dw[0]).then_inc(ld_small, 16)
                sp.dma_start(ident[:, :], t_ident).then_inc(ld_small, 16)
                for t in range(TT):
                    src = x_prompt[0] if t == 0 else x_sample[0, (t - 1) * P:t * P, :]
                    sp.dma_start(xnat[:, t, :], src).then_inc(ld_x[t], 16)
                sp.dma_start(coef[:, :, :], t_coef).then_inc(ld_tab, 16)
                sp.dma_start(logit[:, :], ret_decay_logit.rearrange("a b c -> a (b c)").to_broadcast([P, 8])).then_inc(ld_tab, 16)
                v_unit = lambda n: load_unit(sp, w_in_v[:, :, col(C_V + n * P)], n // 8, 8, n % 8)
                for r in range(8):
                    if r >= 3:
                        sp.wait_ge(wm_used, r - 2)
                    sp.dma_start(wmr[r % 3][:, :, :], wmod_v[:, :, r * 256:(r + 1) * 256]).then_inc(wm_raw[r % 3], 16)
                    if r in V_WITH:
                        v_unit(V_WITH.index(r))
                for n in range(len(V_WITH), 16):
                    v_unit(n)
                sp.wait_ge(h_lo, KB)
                sp.dma_start(rope[:, :, :], t_rope).then_inc(rope_ld, 16)
                with sp.Fori(0, 8) as i:
                    for j in range(2):
                        load_unit(sp, w_in_v[:, :, col(i * 256 + (C_Q + j * P))], i, 2, U_QK + j)
                sp.wait_ge(v_full, 54)
                with sp.Fori(0, 8) as i:
                    for j in range(2):
                        sp.wait_ge(wm_used, i * 2 + (j + 7))
                        sp.dma_start(wmr[3 + j][:, :, :], wmod_v[:, :, col(i * 512 + (2048 + j * 256), 256)]).then_inc(wm_raw[3 + j], 16)
                        load_unit(sp, w_in_v[:, :, col(i * P + (C_U + j * D))], i, 2, U_U + j)
                with sp.Fori(0, 8) as i:
                    for j in range(4):
                        load_unit(sp, w_in_v[:, :, col(i * 256 + (C_RG + (j // 2) * 2 * D + (j % 2) * P))],
                                  i, 4, U_G + j)

            @block.gpsimd
            def _(pool):
                pool.sem_inc(w_split, 2)
                pool.memset(ones[:, :], 1.0)
                pool.memset(ones_mean[:, :], 1.0 / D)
                pool.memset(epsc[:, :], EPS).then_inc(init_ok, 1)
                pool.wait_ge(init_ok, 1)
                with pool.Fori(0, 2) as i:
                    for s in (0, 1):
                        pool.wait_ge(v_full, i * 18 + 9 * (s + 1))
                        if s == 1:
                            pool.wait_ge(xT_st, 16 * KB)
                            pool.wait_ge(h_t, KB)
                        for j in range(4):
                            split_unit(pool, i, 8, 4 * s + j, vsh[s][:, :, j * P:(j + 1) * P],
                                       vsl[s][:, :, j * P:(j + 1) * P])
                with pool.Fori(0, 8) as i:
                    for j in range(2):
                        split_T(pool, i, 2, U_QK + j)
                with pool.Fori(0, 8) as i:
                    for j in range(2):
                        split_T(pool, i, 2, U_U + j)
                pool.wait_ge(h_t, KB)
                pool.memset(ssq[:, :], 0.0).then_inc(cv_ssq, 1)
                with pool.Fori(0, 8) as i:
                    split_T(pool, i, 4, U_G)
                    split_T(pool, i, 4, U_G + 1)
                    pool.wait_ge(cv_ssq, i + 1)
                    pool.wait_ge(cv_sq, i + 1)
                    pool.tensor_tensor(ssq[:, :], ssq[:, :], conv_sq[:, :], ALU.add).then_inc(cv_ssq, 1)
                    split_T(pool, i, 4, U_G + 2)
                    split_T(pool, i, 4, U_G + 3)
                pool.wait_ge(cv_ssq, 9)
                pool.wait_ge(cv_sq, 9)
                pool.tensor_tensor(ssq[:, :], ssq[:, :], conv_sq[:, :], ALU.add).then_inc(cv_ssq, 1)

            @block.scalar
            def _(act):
                act.wait_ge(vec_ok, 2)
                act.activation(small[:, 0:16], vec[:, V_CC:V_CC + 16], ACT.Sigmoid).then_inc(cond_sig, 1)
                for t in range(TT):
                    act.wait_ge(ld_x[t], 16)
                    if t == 0:
                        act.wait_ge(vec_ps, 2)
                        act.wait_ge(vec_ok, 3)
                    else:
                        act.wait_ge(n1_sq, t)
                    act.activation(sqj[:, :], xnat[:, t, :], ACT.Square, scale=1.0 / 32,
                                   accum_out=small[:, 16 + t:17 + t]).then_inc(n1_sq, 1)
                    act.wait_ge(x_tr, 2 * t + 1)
                    act.activation(xT[:, 0:4, t * P:(t + 1) * P],
                                   ps[:, 2 * (t % 3), :].rearrange("p (k n) -> p k n", k=4), ACT.Copy).then_inc(x_cpa, 1)
                act.wait_ge(n1_sq, TT)
                act.wait_ge(init_ok, 1)
                act.activation(small[:, 32:32 + TT], small[:, 16:16 + TT], ACT.Sqrt, bias=epsc[:, :]).then_inc(n1_sqrt, 1)

                def mod_high(slot, turn):
                    act.wait_ge(wm_raw[slot], turn)
                    act.activation(wmh[slot][:, :, :], wmr[slot][:, :, :], ACT.Copy).then_inc(wm_hi, 1)

                mod_high(0, 16)
                mod_high(1, 16)
                act.wait_ge(n1_bc, TT)
                act.activation(g3(ssq[:, :]), psT[0], ACT.Copy).then_inc(n1_ok, 1)
                for r in range(2, 8):
                    mod_high(r % 3, 16 * (r // 3 + 1))
                act.wait_ge(x_cp, TT)
                act.wait_ge(x_cpa, TT)
                for k in range(KB):
                    act.wait_ge(h_t, k + 1)
                    act.wait_ge(mod_ok, 2)
                    hbk = hb[k % 2]
                    act.activation(hbk[:, 0:P], hbk[:, 0:P], ACT.Identity, scale=scale1[:, k, 0:1],
                                   bias=mod[:, M_SH1 + k, 0:1]).then_inc(h_aff, 1)
                    act.activation(hbk[:, P:T], hbk[:, P:T], ACT.Identity, scale=scale1[:, k, 1:2],
                                   bias=mod[:, M_SH1 + k, 1:2]).then_inc(h_aff, 1)
                    act.wait_ge(h_aff, 2 * k + 2)
                    act.activation(x0h[:, k, :], hbk[:, :], ACT.Copy).then_inc(h_hi, 1)
                    act.dma_start(xT_d[k], xT[:, k, :]).then_inc(xT_st, 16)
                def store_v(i):
                    for s in (0, 1):
                        for t in range(TT):
                            n = 9 * s + t
                            act.wait_ge(v_out, i * 18 + (n + 7))
                            act.dma_start(v_d[t, :, col(i * 1024 + s * DV, DV)], vout[n % 2][:, :]).then_inc(v_st[n % 2], 16)

                store_v(0)
                act.wait_ge(xT_st, 16 * KB)
                act.wait_ge(h_t, KB)
                act.wait_ge(x_tr, 2 * TT)
                act.dma_start(diff0[:, :, :], t_diff).then_inc(ld_diff, 16)
                act.wait_ge(dk, 1)
                act.activation(lgt[:, 1, :], lgt[:, 0, :], ACT.Exp, scale=-1.0).then_inc(dka, 1)
                act.wait_ge(dk, 16)
                for dh in range(8):
                    act.activation(dec[:, dh, :], coef[:, dh // 4, :], ACT.Exp, scale=lgt[:, 7, dh:dh + 1]).then_inc(dka, 1)
                act.wait_ge(ld_diff, 16)
                for h in range(H):
                    if h:
                        act.wait_ge(dk, 17 + 3 * h)
                    for d in (0, 1):
                        act.activation(expd[:, d, :], diff0[:, 2 * d, :], ACT.Exp,
                                       scale=lgt[:, 7, 4 * d + h:4 * d + h + 1]).then_inc(dka, 1)
                store_v(1)
                with act.Fori(0, 8) as i:
                    act.wait_ge(p_full, i * 2 + 3)
                    act.wait_ge(rp_out, i * 2 + 2)
                    act.activation(g3(sa[:, :]), psT[0], ACT.Copy).then_inc(p_free[0], 1)
                    for j in (0, 1):
                        act.wait_ge(rp_out, i * 2 + 4)
                        act.dma_start(qk_d[bass.ds(i * 2 + j, 1), :, :].rearrange("a p n -> (a p) n"),
                                      outb[j][:, :]).then_inc(rp_st, 16)
                with act.Fori(0, 8) as i:
                    for j in (0, 1):
                        mod_high(3 + j, i * 16 + 16)
                    act.wait_ge(p_full, i * 2 + (U_U - U_QK + 3))
                    act.wait_ge(glu_ok, i + 1)
                    act.wait_ge(rp_st, 288)
                    act.activation(g3(outb[1][:, :]), psT[0], ACT.Copy).then_inc(p_free[0], 1)
                    act.wait_ge(p_full, i * 2 + (U_U - U_QK + 4))
                    act.activation(g3(outb[0][:, :]), psT[1], ACT.Sigmoid).then_inc(p_free[1], 1)
                with act.Fori(0, 8) as i:
                    for j in range(4):
                        act.wait_ge(gt_st[j % 2], i * 32 + 16 * (j // 2 + 1))
                        if j == 0:
                            act.wait_ge(glu_ok, 9)
                        act.wait_ge(p_full, i * 4 + (U_G - U_QK + j + 3))
                        sg = act.activation(g3(outb[j % 2][:, :]), psT[j % 2], ACT.Sigmoid)
                        sg.then_inc(gt_sig, 1) if j < 2 else sg.then_inc(p_free[j % 2], 1)
                        if j < 2:
                            act.wait_ge(p_free[j], half(i, 4, U_G + j) + 1)
                            dst = s_d[bass.ds(i * 2 + j, 1), :, :]
                        else:
                            act.wait_ge(p_free[j % 2], half(i, 4, U_G + j) + 1)
                            dst = b_d[bass.ds(i * 2 + j - 2, 1), :, :]
                        act.dma_start(dst.rearrange("a p n -> (a p) n"), outb[j % 2][:, :]).then_inc(gt_st[j % 2], 16)
                    act.wait_ge(cv_lat, i * CW + CW)
                    act.wait_ge(cv_ctx, i * (CW - 1) + (CW - 1))
                    act.dma_start(conv_d[bass.ds(i, 1), :, :].rearrange("a p n -> (a p) n"),
                                  conv_acc[:, :]).then_inc(cv_st, 16)
                    act.wait_ge(cv_ssq, i + 2)
                    act.activation(conv_sq[:, :], conv_acc[:, :], ACT.Square).then_inc(cv_sq, 1)
                act.wait_ge(cv_st, 144)
                act.wait_ge(xT_st, 16 * KB)
                for q in (0, 1):
                    act.wait_ge(v_st[q], 16 + 18 * 16)
                    act.wait_ge(gt_st[q], 16 + 16 * 16)

            @block.vector
            def _(dve):
                dve.sem_inc(p_free[0], 1)
                dve.sem_inc(p_free[1], 1)
                dve.sem_inc(v_out, 6)
                dve.sem_inc(rp_out, 2)
                dve.sem_inc(glu_ok, 1)
                dve.sem_inc(rp_st, 32)
                dve.sem_inc(cv_st, 16)
                dve.wait_ge(vec_ps, 1)
                dve.tensor_copy(vec[:, :], ps[:, 6, 0:V_ROWS]).then_inc(vec_ok, 1)
                dve.tensor_copy(identr[:, :], ident[:, :]).then_inc(vec_ok, 1)
                dve.wait_ge(vec_ps, 2)
                dve.tensor_copy(convw[:, :, :], ps[:, 7, 0:KB * CW].rearrange("p (k n) -> p k n", k=KB)).then_inc(vec_ok, 1)
                dve.wait_ge(cond_sig, 1)
                dve.tensor_tensor(cond[:, :, 0], vec[:, V_CC:V_CC + 8], small[:, 0:8], ALU.mult)
                dve.tensor_tensor(cond[:, :, 1], vec[:, V_C:V_C + 8], small[:, 8:16], ALU.mult).then_inc(cond_hi, 1)
                dve.wait_ge(cond_hi, 1)
                dve.tensor_copy(condq[:, :, 0:2], cond[:, :, :]).then_inc(cond_hi, 1)
                dve.tensor_tensor(selT[0:4, :], ident[0:4, 0:2], ident[0:4, 2:4], ALU.add)
                dve.wait_ge(cond_hi, 2)
                dve.tensor_tensor(condq[:, :, 2:4], cond[:, :, :], condq[:, :, 0:2].bitcast(F32), ALU.subtract).then_inc(cond_ok, 1)
                for t in range(TT):
                    dve.wait_ge(x_tr, 2 * t + 2)
                    dve.tensor_copy(xT[:, 4:8, t * P:(t + 1) * P],
                                    ps[:, 2 * (t % 3) + 1, :].rearrange("p (k n) -> p k n", k=4)).then_inc(x_cp, 1)
                dve.wait_ge(n1_sqrt, 1)
                dve.reciprocal(small[:, 48:48 + TT], small[:, 32:32 + TT]).then_inc(n1_rc, 1)
                dve.wait_ge(n1_rc, 1)
                for t in range(TT):
                    if t >= 2:
                        dve.wait_ge(n1_bc, t - 1)
                    dve.tensor_scalar(diag[:, t % 2, :], ident[:, :], small[:, 48 + t:49 + t], None, ALU.mult).then_inc(n1_diag, 1)

                def mod_low(slot, turn):
                    dve.wait_ge(wm_hi, turn)
                    dve.tensor_tensor(wml[slot][:, :, :], wmr[slot][:, :, :], wmh[slot][:, :, :].bitcast(F32),
                                      ALU.subtract).then_inc(wm_lo, 1)

                def norm_x(k):
                    dve.tensor_tensor(hb[k % 2][:, :], xT[:, k, :], ssq[:, :], ALU.mult).then_inc(h_t, 1)

                for r in range(9):
                    if r < 8:
                        mod_low(r % 3, r + 1)
                    if r == 0:
                        dve.wait_ge(n1_ok, 1)
                        dve.wait_ge(x_cp, TT)
                        dve.wait_ge(x_cpa, TT)
                        dve.wait_ge(x_tr, 2 * TT)
                        dve.wait_ge(n1_sq, TT)
                    if r in (1, 2):
                        norm_x(r - 1)
                    if r >= 1:
                        dve.wait_ge(wm_used, r)
                        if r >= 3:
                            dve.wait_ge(mod_col, r - 2)
                        dve.tensor_copy(modrow[0:4, (r - 1) % 2, :], ps[0:4, 5 + (r - 1) % 2, 0:256]).then_inc(mod_row, 1)
                dve.wait_ge(mod_col, 8)
                for q in (0, 1):
                    mo = dve.tensor_tensor(mod[:, 0:16, q], ps[:, 7, 0:32].rearrange("p (m q) -> p m q", q=2)[:, :, q],
                                           vec[:, V_BM:V_BM + 16], ALU.add)
                mo.then_inc(mod_ok, 1)
                dve.wait_ge(mod_ok, 1)
                for q in (0, 1):
                    mo = dve.scalar_tensor_tensor(scale1[:, :, q], mod[:, M_SC1:M_SC1 + 8, q], 1.0,
                                                  vec[:, V_N1:V_N1 + 8], ALU.add, ALU.mult)
                mo.then_inc(mod_ok, 1)
                for k in range(KB + 1):
                    if 2 <= k < KB:
                        dve.wait_ge(h_lo, k - 1)
                        norm_x(k)
                    if k >= 1:
                        dve.wait_ge(h_hi, k)
                        dve.tensor_tensor(x0l[:, k - 1, :], hb[(k - 1) % 2][:, :], x0h[:, k - 1, :].bitcast(F32),
                                          ALU.subtract).then_inc(h_lo, 1)
                def copy_v(i):
                    for s in (0, 1):
                        for t in range(TT):
                            n = 9 * s + t
                            dve.wait_ge(v_full, i * 18 + (n + 19))
                            dve.wait_ge(v_st[n % 2], i * 144 + 16 * (n // 2 + 1))
                            dve.tensor_copy(vout[n % 2][:, :], ps[:, n % 6, :]).then_inc(v_out, 1)

                copy_v(0)
                dve.wait_ge(ld_tab, 32)
                L = lambda r: lgt[:, r, :]
                dve.tensor_scalar(L(1), logit[:, :], -1.0, None, ALU.mult).then_inc(dkm, 1)
                dve.wait_ge(dkm, 1)
                dve.tensor_tensor(L(0), logit[:, :], L(1), ALU.max).then_inc(dk, 1)
                dve.wait_ge(dka, 1)
                dve.tensor_scalar(L(2), L(1), 2.0, None, ALU.add).then_inc(dk, 1)
                dve.wait_ge(dk, 2)
                dve.reciprocal(L(3), L(2)).then_inc(dk, 1)
                dve.wait_ge(dk, 3)
                dve.tensor_tensor(L(4), L(3), L(1), ALU.mult).then_inc(dk, 1)
                dve.wait_ge(dk, 4)
                dve.tensor_tensor(L(5), L(4), L(4), ALU.mult).then_inc(dk, 1)
                dve.wait_ge(dk, 5)
                dve.tensor_scalar(L(6), L(5), 2.0 / 17, 2.0 / 15, ALU.mult, ALU.add).then_inc(dk, 1)
                n = 6
                for q in (13, 11, 9, 7, 5, 3):
                    dve.wait_ge(dk, n)
                    dve.tensor_tensor(L(6), L(6), L(5), ALU.mult).then_inc(dkm, 1)
                    dve.wait_ge(dkm, n - 4)
                    dve.tensor_scalar(L(6), L(6), 2.0 / q, None, ALU.add).then_inc(dk, 1)
                    n += 1
                dve.wait_ge(dk, n)
                dve.tensor_tensor(L(6), L(6), L(5), ALU.mult).then_inc(dk, 1)
                dve.wait_ge(dk, n + 1)
                dve.scalar_tensor_tensor(L(6), L(6), 2.0, L(4), ALU.add, ALU.mult).then_inc(dk, 1)
                dve.tensor_scalar(L(3), logit[:, :], 0.0, None, ALU.min).then_inc(dk, 1)
                dve.wait_ge(dk, n + 3)
                dve.tensor_tensor(L(7), L(3), L(6), ALU.subtract).then_inc(dk, 1)
                assert n + 4 == 16
                dve.wait_ge(dka, 9)
                dve.tensor_scalar(dec[:, :, DKK:DKK + 2], dec[:, :, DKK:DKK + 2], DK ** -0.5, None, ALU.mult).then_inc(dk, 1)
                for h in range(H):
                    dve.wait_ge(dka, 9 + 2 * (h + 1))
                    for d in (0, 1):
                        mk = dve.scalar_tensor_tensor(expd[:, d, :], expd[:, d, :], DK ** -0.5, diff0[:, 2 * d + 1, :],
                                                      ALU.mult, ALU.mult)
                    mk.then_inc(dk, 1)
                    dve.wait_ge(dk, 18 + 3 * h)
                    for jt in (0, 1):
                        x = 128 * (1 - jt)
                        dve.tensor_tensor(masks[:, h, jt, :], expd[:, 0, x:x + 256], expd[:, 1, x:x + 256], ALU.add).then_inc(dk, 1)
                copy_v(1)
                dve.wait_ge(rope_ld, 16)
                with dve.Fori(0, 8) as i:
                    dve.wait_ge(p_free[0], half(i, 2, U_QK) + 1)
                    dve.wait_ge(rp_st, i * 32 + 32)
                    dve.tensor_tensor(outb[0][:, :], sa[:, :], rope[:, 0, :], ALU.mult)
                    dve.tensor_tensor(outb[1][:, :], sa[:, :], rope[:, 1, :], ALU.mult).then_inc(rp_a, 1)
                    dve.wait_ge(p_full, i * 2 + 4)
                    dve.wait_ge(rp_out, i * 2 + 2)
                    dve.tensor_tensor(g3(rt[:, 0, :]), psT[1], g3(rope[:, 1, :]), ALU.mult).then_inc(rp_mul, 1)
                    dve.tensor_tensor(g3(rt[:, 1, :]), psT[1], g3(rope[:, 0, :]), ALU.mult).then_inc(p_free[1], 1)
                    dve.wait_ge(rp_a, i + 1)
                    dve.wait_ge(rp_mul, i + 1)
                    dve.tensor_tensor(outb[0][:, :], outb[0][:, :], rt[:, 0, :], ALU.subtract).then_inc(rp_out, 1)
                    dve.wait_ge(p_free[1], half(i, 2, U_QK + 1) + 1)
                    dve.tensor_tensor(outb[1][:, :], outb[1][:, :], rt[:, 1, :], ALU.add).then_inc(rp_out, 1)
                with dve.Fori(0, 8) as i:
                    for j in (0, 1):
                        mod_low(3 + j, i * 2 + (9 + j))
                    dve.wait_ge(wm_used, i * 2 + 9)
                    dve.wait_ge(mod_col, i * 2 + 8)
                    dve.tensor_copy(modrow[0:4, 0, :], ps[0:4, 6, 0:256]).then_inc(mod_row, 1)
                    dve.wait_ge(p_free[1], half(i, 2, U_U + 1) + 1)
                    dve.wait_ge(p_free[0], half(i, 2, U_U) + 1)
                    dve.tensor_tensor(glu[:, bass.ds(i, 1), :].rearrange("p a n -> p (a n)"), outb[1][:, :],
                                      outb[0][:, :], ALU.mult).then_inc(glu_ok, 1)
                    dve.wait_ge(wm_used, i * 2 + 10)
                    dve.wait_ge(mod_col, i * 2 + 9)
                    dve.tensor_copy(modrow[0:4, 1, :], ps[0:4, 6, 0:256]).then_inc(mod_row, 1)
                dve.wait_ge(mod_col, 25)
                for q in (0, 1):
                    mo = dve.tensor_tensor(mod[:, 16:48, q], ps[:, 7, 32:96].rearrange("p (m q) -> p m q", q=2)[:, :, q],
                                           vec[:, V_BM + 16:V_BM + 48], ALU.add)
                mo.then_inc(mod_ok, 1)
                dve.wait_ge(mod_ok, 3)
                for q in (0, 1):
                    mo = dve.scalar_tensor_tensor(scale2[:, :, q], mod[:, M_SC2:M_SC2 + 8, q], 1.0,
                                                  vec[:, V_N2:V_N2 + 8], ALU.add, ALU.mult)
                mo.then_inc(mod_ok, 1)
                dve.memset(conv_sq[:, :], 0.0).then_inc(cv_sq, 1)

                def retention_gate(i, j):
                    dve.wait_ge(gt_sig, i * 2 + (j + 1))
                    dve.tensor_tensor(g3(outb[j][:, :]), psT[j], g3(outb[j][:, :]), ALU.mult).then_inc(p_free[j], 1)

                def conv_taps(i, taps):
                    for n in taps:
                        s = n - CW // 2 if n <= CW // 2 - 1 else n - CW // 2 + 1
                        w = convw[:, :, :].rearrange("p k n -> p (k n)")[:, bass.ds(i * CW + (s + CW // 2), 1)]
                        row = glu[:, bass.ds(i, 1), :].rearrange("p a n -> p (a n)")
                        a0, a1 = max(0, -s), max(0, s)
                        for lo_, width, sem, per in ((P, GRID_W, cv_lat, CW), (0, P, cv_ctx, CW - 1)):
                            m = width - abs(s)
                            rows_ = NROW if lo_ else 1
                            dst = conv_acc[:, lo_:lo_ + rows_ * width].rearrange("p (r w) -> p r w", w=width)[:, :, a0:a0 + m]
                            src = row[:, lo_:lo_ + rows_ * width].rearrange("p (r w) -> p r w", w=width)[:, :, a1:a1 + m]
                            if sem is cv_lat:
                                dve.wait_ge(cv_lat, i * CW + (n + 1))
                            elif n == 0:
                                dve.wait_ge(cv_lat, i * CW + 1)
                            else:
                                dve.wait_ge(cv_ctx, i * (CW - 1) + n)
                            dve.scalar_tensor_tensor(dst, src, w, dst, ALU.mult, ALU.add).then_inc(sem, 1)

                with dve.Fori(0, 8) as i:
                    dve.wait_ge(cv_st, i * 16 + 16)
                    dve.wait_ge(cv_sq, i + 1)
                    dve.wait_ge(glu_ok, 9)
                    dve.tensor_scalar(conv_acc[:, :], glu[:, bass.ds(i, 1), :].rearrange("p a n -> p (a n)"),
                                      convw[:, :, :].rearrange("p k n -> p (k n)")[:, bass.ds(i * CW + CW // 2, 1)],
                                      vec[:, bass.ds(i + V_CB, 1)], ALU.mult, ALU.add).then_inc(cv_lat, 1)
                    conv_taps(i, range(0, 9))
                    retention_gate(i, 0)
                    conv_taps(i, range(9, 18))
                    retention_gate(i, 1)
                    conv_taps(i, range(18, 30))

            @block.tensor
            def _(pe):
                pe.sem_inc(p_full, 2)
                pe.sem_inc(v_full, 18)
                for q in (0, 1):
                    pe.sem_inc(v_st[q], 16)
                    pe.sem_inc(gt_st[q], 16)
                pe.wait_ge(ld_small, 160)
                pe.transpose(ps[:, 6, 0:V_ROWS], vrows[0:V_ROWS, :], ident[0:V_ROWS, 0:V_ROWS]).then_inc(vec_ps, 1)
                for k in range(KB):
                    mm = pe.transpose(ps[:, 7, k * CW:(k + 1) * CW], dwrows[0:CW, k * P:(k + 1) * P], ident[0:CW, 0:CW])
                mm.then_inc(vec_ps, 1)
                for t in range(TT):
                    pe.wait_ge(ld_x[t], 16)
                    for b in (0, 1):
                        if t >= 3:
                            pe.wait_ge(x_cpa, t - 2) if b == 0 else pe.wait_ge(x_cp, t - 2)
                        for k in range(4):
                            mm = pe.transpose(ps[:, 2 * (t % 3) + b, k * P:(k + 1) * P],
                                              xnat[:, t, (4 * b + k) * P:(4 * b + k + 1) * P], ident[:, :])
                        mm.then_inc(x_tr, 1)
                pe.wait_ge(init_ok, 1)
                pe.wait_ge(x_cpa, TT)
                pe.wait_ge(x_cp, TT)
                for t in range(TT):
                    pe.wait_ge(n1_diag, t + 1)
                    mm = pe.matmul(ps[:, t // 3, (t % 3) * P:(t % 3 + 1) * P], ones[:, :], diag[:, t % 2, :],
                                   start=True, stop=True)
                    mm.then_inc(n1_bc, 1)

                def mod_rows(slot, bank, turn):
                    pe.wait_ge(wm_lo, turn)
                    for k in range(KB):
                        for w in (wmh, wml):
                            mm = pe.matmul(ps[0:4, bank, 0:256], condq[:, k, :], w[slot][:, k, :],
                                           start=(k == 0 and w is wmh), stop=(k == KB - 1 and w is wml))
                    mm.then_inc(wm_used, 1)

                def mod_cols(s, at_, turn):
                    pe.wait_ge(mod_row, turn)
                    for b in (0, 1):
                        mm = pe.matmul(ps[:, 7, at_ + 2 * b:at_ + 2 * b + 2] if isinstance(at_, int) else
                                       ps[:, 7, bass.ds(at_ + 2 * b, 2)],
                                       modrow[0:4, s, b * P:(b + 1) * P], selT[0:4, :], start=True, stop=True)
                    mm.then_inc(mod_col, 1)

                pe.wait_ge(cond_ok, 1)
                pe.wait_ge(vec_ok, 3)
                for r in range(9):
                    if r < 8:
                        if r >= 2:
                            pe.wait_ge(mod_row, r - 1)
                        mod_rows(r % 3, 5 + r % 2, r + 1)
                    if r >= 1:
                        mod_cols((r - 1) % 2, 4 * (r - 1), r)

                pe.wait_ge(n1_ok, 1)
                with pe.Fori(0, 2) as i:
                    for s in (0, 1):
                        pe.wait_ge(w_split, i * 8 + (4 * s + 6))
                        for tiles_ in ((0, 1, 2, 3, 4, 5), (6,), (7,), (8,)) if s == 0 else [(t,) for t in range(TT)]:
                            for k in range(KB):
                                if len(tiles_) > 1:
                                    pe.wait_ge(h_lo, k + 1)
                                for t in tiles_:
                                    n = 9 * s + t
                                    if k == 0:
                                        pe.wait_ge(v_out, i * 18 + (n + 1))
                                    for a, b in ((x0h, vsh), (x0h, vsl), (x0l, vsh)):
                                        mm = pe.matmul(ps[:, n % 6, :], a[:, k, t * P:(t + 1) * P], b[s][:, k, :],
                                                       start=(k == 0 and a is x0h and b is vsh),
                                                       stop=(k == KB - 1 and a is x0l))
                                        if k == KB - 1 and a is x0l:
                                            mm.then_inc(v_full, 1)
                pe.wait_ge(v_out, 42)
                with pe.Fori(0, 8) as i:
                    for j in range(2):
                        unit_T(pe, i, 2, U_QK + j, x0h, x0l)
                with pe.Fori(0, 8) as i:
                    unit_T(pe, i, 2, U_U, x0h, x0l)
                    mod_cols(1, i * 8 + 28, i * 2 + 8)
                    mod_rows(3, 6, i * 2 + 9)
                    unit_T(pe, i, 2, U_U + 1, x0h, x0l)
                    mod_cols(0, i * 8 + 32, i * 2 + 9)
                    mod_rows(4, 6, i * 2 + 10)
                mod_cols(1, 92, 24)
                with pe.Fori(0, 8) as i:
                    for j in range(4):
                        unit_T(pe, i, 4, U_G + j, x0h, x0l)

        tiles, chunk, norm_tiles, o_pe, o_act, o_dve, o_pool = retention_orders()
        PE_, AC, DV_, PO = Order(o_pe), Order(o_act), Order(o_dve), Order(o_pool)
        pe_done, act_done, dve_done, pool_done = S("pe_done"), S("act_done"), S("dve_done"), S("pool_done")
        q_ld, s0_ld, v_ld, g_ld = [S("q_ld0"), S("q_ld1")], S("s0_ld"), [S(f"v_ld{s}") for s in range(3)], [
            S(f"g_ld{s}") for s in range(GP)]
        sp_turn = S("sp_turn")
        g_st, st_st = [S(f"g_st{s}") for s in range(GP)], [S("st_st0"), S("st_st1")]
        vorder = [1, 2, 7, 8, 3, 4, 5, 6, 0]
        kv_bank = lambda d, e: 2 + 2 * d + e
        yorder = [s for s in o_pe if s[0] in ("in", "ia", "tr")]
        y_bank = lambda *s: 6 + yorder.index(s) % 2
        p_slot = {0: 0, 3: 1, 1: 0, 2: 1, 4: 0}

        def y_reader(*s):
            if s[0] == "tr":
                return dve_done, DV_, ("gm", s[1])
            if s == ("ia", 4, 0):
                return act_done, AC, ("yc",)
            if s[0] == "ia":
                return dve_done, DV_, ("ya", s[1], s[2])
            if s[2] < 2:
                return act_done, AC, ("yt", s[1], s[2], s[3])
            return dve_done, DV_, ("ys", s[1], s[2], s[3])

        c_st = at("c_st", [KB, T], X1)
        c_ld = [S(f"c_ld{k}") for k in range(KB)]
        g_uses = [len(range(q, TT, GP)) for q in range(GP)]

        def need(eng, sem, *counts):
            counts = [c for c in counts if c is not None]
            if counts:
                eng.wait_ge(sem, max(counts, key=lambda c: c[0])[1])

        def before(chain, at, step, reader):
            k = chain.index(step)
            found = [(q, 0) for q in chain[:k] if at.has(q)]
            if at.phase != "first":
                found = [(chain[-1], -1)] + found
            if not found:
                return None, None
            sem, order, st = reader(found[-1][0])
            return sem, order.count(at, found[-1][1], st)

        y_steps = lambda step: [q for q in yorder if y_bank(*q) == y_bank(*step)]

        def each(eng, steps, emit, before_last=None):
            def some_of(at):
                for step in steps:
                    if at.has(step):
                        at.late = int(late(step))
                        emit(at, step)
            some_of(At(0, "first"))
            with eng.Fori(1, H) as i:
                some_of(At(i, "all"))
            if before_last is not None:
                before_last()
            some_of(At(H, "last"))

        rms_ps, rms_sqrt, rms_ok = S("rms_ps"), S("rms_sqrt"), S("rms_ok")

        def mean_square(pe):
            for g in range(G3):
                pe.matmul(ps[:, g, 0:GN], ones_mean[:, :], ssq[:, g * GN:(g + 1) * GN], start=True, stop=True).then_inc(rms_ps, 1)

        def root(act, n):
            for g in range(G3):
                act.wait_ge(rms_ps, 3 * n + g - 2)
                act.activation(ssq[:, g * GN:(g + 1) * GN], ps[:, g, 0:GN], ACT.Sqrt, bias=epsc[:, :]).then_inc(rms_sqrt, 1)

        def invert(dve, n):
            for g in range(G3):
                dve.wait_ge(rms_sqrt, 3 * n + g - 2)
                rc = dve.reciprocal(ssq[:, g * GN:(g + 1) * GN], ssq[:, g * GN:(g + 1) * GN])
            rc.then_inc(rms_ok, 1)

        o_sp = [("k", 0), ("k", 1)] + [("v", x) for x in range(3)] + [("gs", x) for x in range(GP)] + [("v", 3)]
        o_sp += [("q", 0), ("q", 1), ("s",)] + [("v", x) for x in range(4, 7)] + [("gs", x) for x in range(GP, TT)]
        o_sp += [("v", x) for x in (7, 8)]

        with nc.Block() as block:
            @block.sync
            def _(sp):
                def load(h, step):
                    k, x = step[0], step[-1]
                    if k in ("k", "q"):
                        need(sp, pool_done, PO.last(h, "ql", x) if k == "k" else None)
                        need(sp, dve_done, None if k == "k" else DV_.this(h, "kl", x))
                        sp.sem_inc(sp_turn, 1)
                        sp.dma_start(qst[x][:, :], qk_d[bass.ds(h.head(2, (8 if k == "k" else 0) + x), 1), :, :].rearrange(
                            "a p n -> (a p) n")).then_inc(q_ld[x], 16)
                    elif k == "s":
                        for d in (0, 1):
                            need(sp, pool_done, PO.last(h, "sl", 1, 3, 1))
                            sp.sem_inc(sp_turn, 1)
                            sp.wait_ge(st_st[d], h.head(16, 16))
                            sp.sem_inc(sp_turn, 1)
                            sp.dma_start(sraw[d][:, :, :], state_ret[0, 0, d, bass.ds(h.head(1, 0), 1), :, :].rearrange(
                                "a (k p) n -> p (a k) n", p=P)).then_inc(s0_ld, 16)
                    elif k == "v":
                        t = vorder[x]
                        need(sp, pool_done, PO.last(h, "vl", x + 6) if x < 3 else PO.this(h, "vl", x - 3))
                        sp.sem_inc(sp_turn, 1)
                        sp.dma_start(vst[x % 3][:, :], v_d[t, :, bass.ds(h.head(DV, 0), DV)]).then_inc(v_ld[x % 3], 16)
                    else:
                        t, q = norm_tiles[x], x % GP
                        sp.wait_ge(g_st[q], h.head(16 * g_uses[q], 16 * (x // GP + 1)))
                        sp.sem_inc(sp_turn, 1)
                        sp.dma_start(gp[q][:, :, :], s_d[bass.ds(h.head(4, 0), 4), :, t * P:(t + 1) * P].rearrange(
                            "a p n -> p a n")).then_inc(g_ld[q], 16)

                def first_of_block3():
                    for j in (0, 1):
                        load_unit(sp, wsrc(w_conv_out)[:, :, j * P:(j + 1) * P], 0, 2, U_CONV + j)

                each(sp, o_sp, load, first_of_block3)
                at_end = At(H, "last")
                at_end.late = 1
                need(sp, pe_done, PE_.this(at_end, "in", 1, 3, 1))
                for k in range(KB):
                    if k == KB - 1:
                        sp.wait_ge(st_st[0], 16 + H * 16)
                    sp.dma_start(c_st[:, k, :], conv_d[k]).then_inc(c_ld[k], 16)

            @block.gpsimd
            def _(pool):
                for q in range(GP):
                    pool.sem_inc(g_st[q], 16)
                for d in (0, 1):
                    pool.sem_inc(st_st[d], 16)
                pool.sem_inc(pool_done, PO.start)

                def low(h, step):
                    if step[0] == "vl":
                        x = step[1]
                        need(pool, act_done, AC.this(h, "vh", x))
                        pool.tensor_tensor(vl[:, vorder[x], :], vst[x % 3][:, :], vh[:, vorder[x], :].bitcast(F32),
                                           ALU.subtract).then_inc(pool_done, PO.one(h, *step))
                    elif step[0] == "ql":
                        x = step[1]
                        need(pool, act_done, AC.this(h, "qh", x))
                        pool.tensor_tensor(ql[:, x, :], qst[x][:, :], qh[:, x, :].bitcast(F32),
                                           ALU.subtract).then_inc(pool_done, PO.one(h, *step))
                    else:
                        _, d, t, e = step
                        need(pool, act_done, AC.this(h, "sh", d, t, e))
                        pool.tensor_tensor(stl[d][t % 2][:, e, :], sraw[d][:, e, :], sth[d][t % 2][:, e, :].bitcast(F32),
                                           ALU.subtract).then_inc(pool_done, PO.one(h, *step))

                each(pool, o_pool, low)
                for j in (0, 1):
                    split_T(pool, 0, 2, U_CONV + j)

            @block.scalar
            def _(act):
                act.sem_inc(act_done, AC.start)
                root(act, 1)

                def act_step(h, step):
                    k, a = step[0], step[1:]
                    if k in ("kh", "qh"):
                        p = a[0]
                        act.wait_ge(q_ld[p], h.head(32, 16 if k == "kh" else 32))
                        need(act, pe_done, PE_.last(h, "sc", 4) if k == "kh" else PE_.last(h, "in", 1, 3, 1))
                        need(act, pool_done, PO.last(h, "ql", 1))
                        ins = act.activation((kh if k == "kh" else qh)[:, p, :], qst[p][:, :], ACT.Copy)
                    elif k == "vh":
                        x = a[0]
                        act.wait_ge(v_ld[x % 3], h.head(48, 16 * (x // 3 + 1)))
                        if vorder[x] == 0:
                            need(act, pe_done, PE_.last(h, "kv", 1, 3, 1),
                                 PE_.last(h, "ia", 4, 0))
                        else:
                            need(act, pe_done, PE_.last(h, "kv", 1, 2, 1),
                                 PE_.last(h, "ia", 2, 1))
                        ins = act.activation(vh[:, vorder[x], :], vst[x % 3][:, :], ACT.Copy)
                    elif k == "knh":
                        d, t, x = a
                        used = (PE_.this(h, "kv", x, 2, 1) if d == 2 else PE_.this(h, "kv", d, t - 1, 1) if t else
                                PE_.last(h, "kv", d, 3, 1))
                        need(act, pe_done, PE_.this(h, "kn", d, t), used)
                        need(act, dve_done, DV_.this(h, "dcl" if d == 2 else "dec"))
                        if d == 2:
                            ins = act.activation(knh[x][:, 0, :], ps[:, 0, 0:DK], ACT.Copy,
                                                 scale=dechl[:, x, DKK + (1 - x):DKK + 2 - x])
                        else:
                            ins = act.activation(knh[d][:, x, :], ps[:, 0, x * DK:(x + 1) * DK], ACT.Copy,
                                                 scale=dech[:, d, DKK + x:DKK + x + 1])
                    elif k == "ph":
                        cc = a[0]
                        need(act, dve_done, DV_.this(h, "pm", cc))
                        used = {0: lambda: PE_.last(h, "ia", 4, 0), 3: lambda: PE_.last(h, "ia", 2, 1), 1: lambda: PE_.this(h, "ia", 0, 1),
                                2: lambda: PE_.this(h, "ia", 3, 1), 4: lambda: PE_.this(h, "ia", 1, 1)}[cc]()
                        need(act, pe_done, used)
                        s = p_slot[cc]
                        ins = act.activation(ph[s][:, 0, 0:P] if cc == 4 else ph[s][:, :, :],
                                             p32[:, 0, 0:P] if cc == 4 else p32[:, :, :], ACT.Copy)
                    elif k == "sh":
                        d, t, e = a
                        if t == 0:
                            act.wait_ge(s0_ld, h.head(32, 32))
                            need(act, pe_done, PE_.last(h, "in", d, 2, 1))
                        else:
                            need(act, dve_done, DV_.this(h, "su", d, t, e))
                            if t >= 2:
                                need(act, pe_done, PE_.this(h, "in", d, t - 2, 1))
                            else:
                                need(act, pe_done, PE_.last(h, "in", d, 3, 1))
                        ins = act.activation(sth[d][t % 2][:, e, :], sraw[d][:, e, :], ACT.Copy)
                    elif k == "yt":
                        d, t, x = a
                        s = ("in", d, t, x)
                        need(act, pe_done, PE_.this(h, *s),
                             PE_.last(h, "tr", norm_tiles.index(tiles(chunk(d, t))[x])))
                        ins = act.activation(yb[:, tiles(chunk(d, t))[x], :], ps[:, y_bank(*s), :], ACT.Copy,
                                             scale=dech[:, d, DQ + x:DQ + x + 1])
                    elif k == "yc":
                        need(act, pe_done, PE_.this(h, "ia", 4, 0),
                             PE_.last(h, "tr", TT - 1))
                        ins = act.activation(yb[:, 0, :], ps[:, y_bank("ia", 4, 0), :], ACT.Copy)
                    elif k == "so":
                        d, e = a
                        need(act, pe_done, PE_.this(h, "kv", d, 3, e))
                        need(act, pool_done, PO.this(h, "sl", d, 3, e))
                        ins = act.activation(sraw[d][:, e, :], ps[:, kv_bank(d, e), :], ACT.Copy)
                    elif k == "sq":
                        need(act, dve_done, DV_.this(h, "ag", TT - 1))
                        ins = act.activation(rst[:, :], bag[:, :, 1], ACT.Sqrt, bias=epsc[:, :])
                    elif k == "yna":
                        n, t = a[0], norm_tiles[a[0]]
                        need(act, dve_done, DV_.this(h, "nm"))
                        ins = act.activation(yb[:, t, :], yb[:, t, :], ACT.Identity, scale=rst[:, n:n + 1], bias=nmr[:, n:n + 1])
                    else:
                        n, t = a[0], norm_tiles[a[0]]
                        need(act, dve_done, DV_.this(h, "gm", n))
                        act.dma_start(g_d[bass.ds(h.head(4, 0), 4), :, t * P:(t + 1) * P].rearrange("a p n -> p a n"),
                                      gp[n % GP][:, :, :]).then_inc(g_st[n % GP], 16)
                        return
                    ins.then_inc(act_done, AC.one(h, *step))
                    if k == "so" and a[1] == 1:
                        need(act, act_done, AC.this(h, *step))
                        act.dma_start(new_state[0, 0, a[0], bass.ds(h.head(1, 0), 1), :, :].rearrange("a (k p) n -> p (a k) n", p=P),
                                      sraw[a[0]][:, :, :]).then_inc(st_st[a[0]], 16)

                each(act, o_act, act_step)

            @block.vector
            def _(dve):
                dve.sem_inc(dve_done, DV_.start)
                mrows = masks[:, :, :, :].rearrange("p h a n -> p h (a n)")
                decv = dec[:, :, :].rearrange("p (d h) n -> p h d n", d=2)

                def dve_step(h, step):
                    k, a = step[0], step[1:]
                    if k in ("dec", "dcl"):
                        if k == "dec":
                            need(dve, act_done, AC.last(h, "yt", 1, 1, 1),
                                 AC.last(h, "knh", 1, 2, 1))
                            need(dve, dve_done, DV_.last(h, "su", 1, 2, 1),
                                 DV_.last(h, "knl", 1, 2, 1))
                        else:
                            need(dve, act_done, AC.last(h, "knh", 2, 0, 1))
                            need(dve, dve_done, DV_.last(h, "ys", 1, 3, 1))
                        ins = dve.tensor_scalar((dech if k == "dec" else dechl)[:, :, :],
                                                decv[:, bass.ds(h.head(1, 0), 1), :, :].rearrange("p a d n -> p (a d) n"),
                                                1.0, None, ALU.mult)
                    elif k == "mask":
                        need(dve, dve_done, DV_.last(h, "pm", 4))
                        ins = dve.tensor_scalar(maskh[:, :, :].rearrange("p a n -> p (a n)"),
                                                mrows[:, bass.ds(h.head(1, 0), 1), :].rearrange("p a n -> p (a n)"),
                                                1.0, None, ALU.mult)
                    elif k == "sep":
                        need(dve, dve_done, DV_.this(h, "st", TT - 1))
                        dve.sem_inc(dve_done, DV_.one(h, *step))
                        return
                    elif k == "kl":
                        p = a[0]
                        need(dve, act_done, AC.this(h, "kh", p))
                        ins = dve.tensor_tensor(kl[:, p, :], qst[p][:, :], kh[:, p, :].bitcast(F32), ALU.subtract)
                    elif k == "knl":
                        d, t, x = a
                        need(dve, act_done, AC.this(h, "knh", d, t, 1))
                        need(dve, dve_done, DV_.this(h, "dcl" if d == 2 else "dec"))
                        if d == 2:
                            ins = dve.scalar_tensor_tensor(knl[x][:, 0, :], ps[:, 0, 0:DK], dechl[:, x, DKK + (1 - x):DKK + 2 - x],
                                                           knh[x][:, 0, :].bitcast(F32), ALU.mult, ALU.subtract)
                        else:
                            ins = dve.scalar_tensor_tensor(knl[d][:, x, :], ps[:, 0, x * DK:(x + 1) * DK],
                                                           dech[:, d, DKK + x:DKK + x + 1], knh[d][:, x, :].bitcast(F32),
                                                           ALU.mult, ALU.subtract)
                    elif k == "pm":
                        cc = a[0]
                        need(dve, pe_done, PE_.this(h, "sc", cc))
                        prev = {0: lambda: DV_.last(h, "pl", 4), 3: lambda: DV_.this(h, "pl", 0),
                                1: lambda: DV_.this(h, "pl", 3), 2: lambda: DV_.this(h, "pl", 1),
                                4: lambda: DV_.this(h, "pl", 2)}[cc]()
                        need(dve, dve_done, prev,
                             DV_.this(h, "mask"))
                        n = P if cc == 4 else 512
                        flat = lambda t_: t_[:, :, :].rearrange("p a n -> p (a n)")[:, 0:n]
                        ins = dve.tensor_tensor(flat(p32), ps[:, 1, 0:n], flat(maskh), ALU.mult)
                    elif k == "pl":
                        cc = a[0]
                        need(dve, act_done, AC.this(h, "ph", cc))
                        n = P if cc == 4 else 512
                        s = p_slot[cc]
                        flat = lambda t_: t_[:, :, :].rearrange("p a n -> p (a n)")[:, 0:n]
                        ins = dve.tensor_tensor(flat(pl[s]), flat(p32), flat(ph[s]).bitcast(F32), ALU.subtract)
                    elif k == "su":
                        d, t, e = a
                        need(dve, pe_done, PE_.this(h, "kv", d, t - 1, e))
                        need(dve, pool_done, PO.this(h, "sl", d, t - 1, e))
                        need(dve, dve_done, DV_.this(h, "dcl" if t == 3 else "dec"))
                        ins = dve.scalar_tensor_tensor(sraw[d][:, e, :], sraw[d][:, e, :], (dechl if t == 3 else dech)[:, d, DS:DS + 1],
                                                       ps[:, kv_bank(d, e), :], ALU.mult, ALU.add)
                    elif k == "ya":
                        s = ("ia",) + a
                        need(dve, pe_done, PE_.this(h, *s))
                        t = tiles(a[0])[a[1]]
                        d0, t0 = (0, a[0]) if a[0] < 2 else (1, 3 - a[0])
                        need(dve, act_done, AC.this(h, "yt", d0, t0, a[1]))
                        ins = dve.tensor_tensor(yb[:, t, :], yb[:, t, :], ps[:, y_bank(*s), :], ALU.add)
                    elif k == "ys":
                        d, t, x = a
                        s = ("in",) + a
                        cc = chunk(d, t)
                        need(dve, pe_done, PE_.this(h, *s))
                        need(dve, dve_done, DV_.this(h, "ya", cc, x))
                        ins = dve.scalar_tensor_tensor(yb[:, tiles(cc)[x], :], ps[:, y_bank(*s), :], dechl[:, d, DQ + x:DQ + x + 1],
                                                       yb[:, tiles(cc)[x], :], ALU.mult, ALU.add)
                    elif k in ("st", "ag"):
                        n, t = a[0], norm_tiles[a[0]]
                        if k == "ag":
                            ins = dve.bn_aggr(bag[:, n, :], bst[:, n, :])
                        else:
                            if t == 0:
                                need(dve, act_done, AC.this(h, "yc"))
                            else:
                                cc, x = (t - 1) // 2, (t - 1) % 2
                                dd, t2 = (0, cc) if cc >= 2 else (1, 3 - cc)
                                need(dve, dve_done, DV_.this(h, "ys", dd, t2, x))
                            need(dve, dve_done, DV_.last(h, "ag", n))
                            ins = dve.bn_stats(bst[:, n, :], yb[:, t, :])
                    elif k == "rc":
                        need(dve, act_done, AC.this(h, "sq"))
                        ins = dve.reciprocal(rst[:, :], rst[:, :])
                    elif k == "nm":
                        need(dve, dve_done, DV_.this(h, "rc"))
                        ins = dve.scalar_tensor_tensor(nmr[:, :], bag[:, :, 0], -1.0, rst[:, :], ALU.mult, ALU.mult)
                    elif k == "yn":
                        n, t = a[0], norm_tiles[a[0]]
                        need(dve, dve_done, DV_.this(h, "rc"))
                        ins = dve.tensor_scalar(yb[:, t, :], yb[:, t, :], bag[:, n, 0:1], rst[:, n:n + 1],
                                                ALU.subtract, ALU.mult)
                    elif k == "gm":
                        n = a[0]
                        q = n % GP
                        dve.wait_ge(g_ld[q], h.head(16 * g_uses[q], 16 * (n // GP + 1)))
                        need(dve, pe_done, PE_.this(h, "tr", n))
                        ins = dve.tensor_tensor(gp[q][:, :, :], gp[q][:, :, :],
                                                ps[:, y_bank("tr", n), :].rearrange("p (a n) -> p a n", a=4), ALU.mult)
                    ins.then_inc(dve_done, DV_.one(h, *step))
                    if step == ("ya", 2, 1) and h.phase == "first":
                        invert(dve, 1)

                each(dve, o_dve, dve_step)

            @block.tensor
            def _(pe):
                pe.sem_inc(pe_done, PE_.start)
                mean_square(pe)
                pe.wait_ge(rms_sqrt, 3)
                kn_steps = [s for s in o_pe if s[0] == "kn"]
                sc_steps = [s for s in o_pe if s[0] == "sc"]

                def pe_step(h, step):
                    def three(out, a, b, first=True, last=True):
                        pe.matmul(out, a[0], b[0], start=first, stop=False)
                        pe.matmul(out, a[0], b[1], start=False, stop=False)
                        return pe.matmul(out, a[1], b[0], start=False, stop=last)

                    k, a = step[0], step[1:]
                    if k == "kn":
                        d, t = a
                        read = before(kn_steps, h, step, lambda q: (dve_done, DV_, ("knl",) + q[1:] + (1,)))
                        need(pe, dve_done, DV_.this(h, "kl", 1), read[1])
                        tl = (0,) if d == 2 else tiles(chunk(d, t))
                        for x, tt in enumerate(tl):
                            for e in (0, 1):
                                out = ps[:, 0, x * DK + e * P:x * DK + (e + 1) * P]
                                pe.matmul(out, kh[:, e, tt * P:(tt + 1) * P], identr[:, :], start=True, stop=False)
                                mm = pe.matmul(out, kl[:, e, tt * P:(tt + 1) * P], identr[:, :], start=False, stop=True)
                    elif k == "sc":
                        cc = a[0]
                        read = before(sc_steps, h, step, lambda q: (dve_done, DV_, ("pm",) + q[1:]))
                        need(pe, pool_done, PO.this(h, "ql", 1))
                        need(pe, dve_done, read[1])
                        if cc == 4:
                            for e in (0, 1):
                                mm = three(ps[:, 1, 0:P], (kh[:, e, 0:P], kl[:, e, 0:P]), (qh[:, e, 0:P], ql[:, e, 0:P]),
                                           e == 0, e == 1)
                        else:
                            t0 = tiles(cc)[0]
                            qs = slice(t0 * P, (t0 + 2) * P)
                            for x in (0, 1):
                                ks = slice((t0 + x) * P, (t0 + x + 1) * P)
                                for e in (0, 1):
                                    mm = three(ps[:, 1, x * 256:(x + 1) * 256], (kh[:, e, ks], kl[:, e, ks]),
                                               (qh[:, e, qs], ql[:, e, qs]), e == 0, e == 1)
                    elif k == "kv":
                        d, t, e = a
                        tl = (0,) if t == 3 else tiles(chunk(d, t))
                        if t == 3:
                            need(pe, dve_done, DV_.this(h, "knl", 2, 0, d),
                                 DV_.this(h, "su", d, 3, e))
                        else:
                            need(pe, dve_done, DV_.this(h, "knl", d, t, 1), DV_.this(h, "su", d, t, e) if t else None)
                            if t == 0:
                                need(pe, act_done, AC.last(h, "so", d, e))
                        need(pe, pool_done, PO.this(h, "vl", max(vorder.index(tt) for tt in tl)))
                        for x, tt in enumerate(tl):
                            mm = three(ps[:, kv_bank(d, e), :], [z[d][:, x, e * P:(e + 1) * P] for z in (knh, knl)],
                                       (vh[:, tt, :], vl[:, tt, :]), x == 0, x == len(tl) - 1)
                    elif k in ("in", "ia"):
                        rsem, read = before(y_steps(step), h, step, lambda q: y_reader(*q))
                        need(pe, act_done, read if rsem is act_done else None)
                        need(pe, dve_done, read if rsem is dve_done else None,
                             None if k == "in" else DV_.this(h, "pl", a[0]))
                        out = ps[:, y_bank(*step), :]
                        if k == "in":
                            d, t, x = a
                            need(pe, pool_done, PO.this(h, "sl", d, t, 1), PO.this(h, "ql", 1))
                            tt = tiles(chunk(d, t))[x]
                            for e in (0, 1):
                                mm = three(out, [z[:, e, tt * P:(tt + 1) * P] for z in (qh, ql)],
                                           [z[d][t % 2][:, e, :] for z in (sth, stl)], e == 0, e == 1)
                        else:
                            cc, x = a
                            s = p_slot[cc]
                            tl = (0,) if cc == 4 else tiles(cc)
                            need(pe, pool_done, PO.this(h, "vl", max(vorder.index(tt) for tt in tl)))
                            for j, tt in enumerate(tl):
                                mm = three(out, [z[s][:, j, x * P:(x + 1) * P] for z in (ph, pl)],
                                           (vh[:, tt, :], vl[:, tt, :]), j == 0, j == len(tl) - 1)
                    else:
                        n, t = a[0], norm_tiles[a[0]]
                        rsem, read = before(y_steps(step), h, step, lambda q: y_reader(*q))
                        need(pe, act_done, read if rsem is act_done else None, AC.this(h, "yna", n) if n % 2 else None)
                        need(pe, dve_done, read if rsem is dve_done else None, None if n % 2 else DV_.this(h, "yn", n))
                        for e in range(4):
                            mm = pe.transpose(ps[:, y_bank("tr", n), e * P:(e + 1) * P], yb[:, t, e * P:(e + 1) * P], ident[:, :])
                    mm.then_inc(pe_done, PE_.one(h, *step))

                each(pe, o_pe, pe_step)

        c_sg = at("c_sg", [2, T], XA)
        ob = at("ob", [TT, D], X0)
        fg = at("fg", [KB, T], X0 + 8 * BLK)
        c_n, c_sig, c_z, c_hi, c_lo = S("c_n"), S("c_sig"), S("c_z"), S("c_hi"), S("c_lo")
        ga_ld, gr_ld, g_hi, g_lo = S("ga_ld"), S("gr_ld"), S("g_hi"), S("g_lo")
        ev = S("ev")
        cb_hi, cb_lo = S("cb_hi"), S("cb_lo")
        sq_ok, sq_add = S("sq_ok"), S("sq_add")
        h2_t, h2_aff, h2_hi, h2_lo = S("h2_t"), S("h2_aff"), S("h2_hi"), S("h2_lo")
        m_sq, m_hi, m_lo = S("m_sq"), S("m_hi"), S("m_lo")
        f_n, o_trl, o_trr, o_cpa, o_cpd, o_st = S("f_n"), S("o_trl"), S("o_trr"), S("o_cpa"), S("o_cpd"), S("o_st")
        blk = lambda d_, i: d_[bass.ds(i, 1), :, :].rearrange("a p n -> (a p) n")
        brow = lambda t_, i: t_[:, bass.ds(i, 1), :].rearrange("p a n -> p (a n)")
        parts = lambda slot: [(ps[:, 3 * slot, 0:P], slice(0, P), 0), (ps[:, 3 * slot, P:GN], slice(P, GN), 1),
                              (ps[:, 3 * slot + 1:3 * slot + 3, 0:GN], slice(GN, T), 1)]
        two = lambda t_, sl: t_.rearrange("p (g n) -> p g n", g=2) if sl.start == GN else t_
        branch = [(U_CONV, wsrc(w_conv_out)), (U_RET, wsrc(w_ret_out)), (U_RET + 8, wsrc(w_ret_out, D)), (U_OUT, wsrc(w_out))]
        w2_v = w_mlp2[0].rearrange("(q k p) n -> q p k n", k=KB, p=P)

        with nc.Block() as block:
            @block.sync
            def _(sp):
                for j in range(2, 8):
                    load_unit(sp, branch[0][1][:, :, j * P:(j + 1) * P], 0, 2, U_CONV + j)
                for u0, src in branch[1:]:
                    with sp.Fori(0, 4) as i:
                        for j in range(2):
                            load_unit(sp, src[:, :, col(i * 256 + j * P)], i, 2, u0 + j)
                with sp.Fori(0, 4) as i:
                    for j in range(8):
                        load_unit(sp, wsrc(w_mlp1)[:, :, col(i * D + j * P)], i, 16, U_MLP + j)
                    for j in range(8):
                        load_unit(sp, w2_v[bass.ds(i, 1), :, :, j * P:(j + 1) * P].rearrange("q p k n -> p (q k) n"),
                                  i, 16, U_MLP + 8 + j)
                for t in range(TT):
                    sp.wait_ge(o_cpa, t + 1)
                    sp.wait_ge(o_cpd, t + 1)
                    dst = y_prompt[0] if t == 0 else y_sample[0, (t - 1) * P:t * P, :]
                    sp.dma_start(dst, ob[:, t, :]).then_inc(o_st, 16)
                sp.wait_ge(o_st, 16 * TT)

            @block.gpsimd
            def _(pool):
                for k in range(KB):
                    pool.wait_ge(c_hi, k + 1)
                    pool.tensor_tensor(x0l[:, k, :], c_st[:, k, :], x0h[:, k, :].bitcast(F32), ALU.subtract).then_inc(c_lo, 1)
                for j in range(2, 8):
                    split_T(pool, 0, 2, U_CONV + j)
                for u0, _s in branch[1:]:
                    with pool.Fori(0, 4) as i:
                        for j in range(2):
                            split_T(pool, i, 2, u0 + j)
                with pool.Fori(0, 4) as i:
                    for j in range(16):
                        split_T(pool, i, 16, U_MLP + j)
                for k in range(KB - 1):
                    pool.wait_ge(sq_ok, 9 + k)
                    pool.wait_ge(sq_add, 10 + k)
                    pool.tensor_tensor(ssq[:, :], ssq[:, :], stage[k % 2][:, :], ALU.add).then_inc(sq_add, 1)

            def unit_full(i, per, c):
                return i * per + (c - U_QK + 3)

            @block.scalar
            def _(act):
                for k in range(KB + 1):
                    if k < KB:
                        act.wait_ge(c_n, k + 1)
                        if k >= 2:
                            act.wait_ge(c_z, k - 1)
                        act.activation(c_sg[:, k % 2, :], c_st[:, k, :], ACT.Sigmoid,
                                       scale=vec[:, V_CG + k:V_CG + k + 1]).then_inc(c_sig, 1)
                    if k >= 1:
                        act.wait_ge(c_z, k)
                        act.activation(x0h[:, k - 1, :], c_st[:, k - 1, :], ACT.Copy).then_inc(c_hi, 1)
                act.wait_ge(c_lo, KB)
                for q in range(GP):
                    act.wait_ge(g_st[q], 16 + g_uses[q] * H * 16)
                for q in (0, 1):
                    act.wait_ge(st_st[q], 16 + H * 16)
                for r, (xh, rows, gates) in enumerate(((x1h, 0, 0), (x0h, 8, 8))):
                    if r == 1:
                        act.wait_ge(p_full, unit_full(0, 2, U_CONV + 7))
                    with act.Fori(0, 4) as i:
                        for j in range(2):
                            act.wait_ge(ev, i * 2 + (8 * r + j + 1))
                            act.dma_start(stage[1][:, :], blk(b_d, i * 2 + (gates + j))).then_inc(ga_ld, 16)
                            act.wait_ge(g_lo, i * 2 + (8 * r + j + 1))
                            act.dma_start(stage[0][:, :], blk(g_d, i * 2 + (rows + j))).then_inc(gr_ld, 16)
                            act.wait_ge(gr_ld, i * 32 + 16 * (8 * r + j + 1))
                            act.activation(brow(xh, i * 2 + j), stage[0][:, :], ACT.Copy).then_inc(g_hi, 1)
                act.wait_ge(p_full, unit_full(0, 2, U_RET + 7))
                with act.Fori(0, 4) as i:
                    for j in range(2):
                        act.wait_ge(ev, i * 2 + (16 + j + 1))
                        act.dma_start(stage[1][:, :], blk(b_d, i * 2 + (8 + j))).then_inc(ga_ld, 16)
                        act.wait_ge(ev, i * 2 + (16 + j + 2))
                        act.activation(brow(x1h, i * 2 + j), brow(acc, i * 2 + j), ACT.Copy).then_inc(cb_hi, 1)
                act.wait_ge(g_lo, 17)
                with act.Fori(0, 4) as i:
                    for j in range(2):
                        act.wait_ge(p_free[1 - j], half(i, 2, U_OUT + j - 1) + 1)
                        act.wait_ge(ev, 25)
                        act.dma_start(stage[1][:, :], blk(xT_d, i * 2 + j)).then_inc(ga_ld, 16)
                        act.wait_ge(p_free[j], half(i, 2, U_OUT + j) + 1)
                        act.wait_ge(sq_add, i * 2 + (j + 1))
                        act.activation(stage[0][:, :], brow(acc, i * 2 + j), ACT.Square).then_inc(sq_ok, 1)
                root(act, 2)
                for k in range(KB):
                    act.wait_ge(h2_t, k + 1)
                    st = stage[k % 2]
                    for q, sl in ((0, slice(0, P)), (1, slice(P, T))):
                        act.activation(st[:, sl], st[:, sl], ACT.Identity, scale=scale2[:, k, q:q + 1],
                                       bias=mod[:, M_SH2 + k, q:q + 1]).then_inc(h2_aff, 1)
                    act.wait_ge(h2_aff, 2 * k + 2)
                    act.activation(x0h[:, k, :], st[:, :], ACT.Copy).then_inc(h2_hi, 1)
                act.wait_ge(h2_lo, KB)
                with act.Fori(0, 4) as i:
                    act.wait_ge(p_full, unit_full(i, 16, U_MLP - 1))
                    for j in range(8):
                        act.wait_ge(p_full, unit_full(i, 16, U_MLP + j))
                        act.wait_ge(m_lo, i * 8 + (j + 1))
                        act.activation(g3(stage[j % 2][:, :]), psT[j % 2], ACT.Relu).then_inc(p_free[j % 2], 1)
                        act.wait_ge(m_sq, i * 8 + (j + 1))
                        act.activation(x1h[:, j, :], stage[j % 2][:, :], ACT.Copy).then_inc(m_hi, 1)
                act.wait_ge(m_lo, 34)
                for k in range(KB):
                    act.wait_ge(p_free[k % 2], half(3, 16, U_MLP + 8 + k) + 1)
                    if k >= 2:
                        act.wait_ge(sq_add, 9 + k)
                    act.activation(stage[k % 2][:, :], acc[:, k, :], ACT.Square).then_inc(sq_ok, 1)
                    act.activation(fg[:, k, :], acc[:, k, :], ACT.Copy, scale=vec[:, V_FG + k:V_FG + k + 1]).then_inc(f_n, 1)
                act.wait_ge(rms_ps, 7)
                act.activation(small[:, 32:32 + TT], ps[:, 6, 0:TT], ACT.Sqrt, bias=epsc[:, :]).then_inc(rms_sqrt, 1)
                act.wait_ge(rms_ok, 3)
                for t in range(TT):
                    act.wait_ge(o_trl, t + 1)
                    act.activation(ob[:, t, 0:512], ps[:, t % 3, :], ACT.Copy, scale=small[:, 48 + t:49 + t]).then_inc(o_cpa, 1)

            @block.vector
            def _(dve):
                dve.sem_inc(m_lo, 2)
                dve.sem_inc(ev, 1)
                dve.sem_inc(g_lo, 1)

                dve.wait_ge(rms_ok, 1)
                for k in range(KB + 1):
                    if k < KB:
                        dve.wait_ge(c_ld[k], 16)
                        dve.tensor_tensor(c_st[:, k, :], c_st[:, k, :], ssq[:, :], ALU.mult).then_inc(c_n, 1)
                    if k >= 1:
                        dve.wait_ge(c_sig, k)
                        dve.scalar_tensor_tensor(c_st[:, k - 1, :], c_st[:, k - 1, :], vec[:, V_CG + k - 1:V_CG + k],
                                                 c_sg[:, (k - 1) % 2, :], ALU.mult, ALU.mult).then_inc(c_z, 1)
                dve.wait_ge(c_lo, KB)
                for r, xl in enumerate((x1l, x0l, None)):
                    if r == 1:
                        dve.wait_ge(p_full, unit_full(0, 2, U_CONV + 7))
                    with dve.Fori(0, 4) as i:
                        for j in range(2):
                            if r < 2:
                                dve.wait_ge(g_hi, i * 2 + (8 * r + j + 1))
                                xh = (x1h, x0h)[r]
                                dve.tensor_tensor(brow(xl, i * 2 + j), stage[0][:, :], brow(xh, i * 2 + j).bitcast(F32),
                                                  ALU.subtract).then_inc(g_lo, 1)
                            dve.wait_ge(p_full, unit_full(i, 2, U_CONV + 8 * r + j))
                            dve.wait_ge(ga_ld, i * 32 + 16 * (8 * r + j + 1))
                            dve.tensor_tensor(g3(stage[1][:, :]), psT[j], g3(stage[1][:, :]), ALU.mult).then_inc(p_free[j], 1)
                            dve.wait_ge(p_free[j], half(i, 2, U_CONV + 8 * r + j) + 1)
                            if r == 0:
                                dve.tensor_scalar(brow(acc, i * 2 + j), stage[1][:, :], 1.0, None, ALU.mult).then_inc(ev, 1)
                            else:
                                dve.tensor_tensor(brow(acc, i * 2 + j), brow(acc, i * 2 + j), stage[1][:, :], ALU.add).then_inc(ev, 1)
                            if r == 2:
                                dve.wait_ge(cb_hi, i * 2 + (j + 1))
                                dve.tensor_tensor(brow(x1l, i * 2 + j), brow(acc, i * 2 + j), brow(x1h, i * 2 + j).bitcast(F32),
                                                  ALU.subtract).then_inc(cb_lo, 1)
                dve.memset(ssq[:, :], 0.0).then_inc(sq_add, 1)
                with dve.Fori(0, 4) as i:
                    for j in range(2):
                        dve.wait_ge(p_full, unit_full(i, 2, U_OUT + j))
                        dve.wait_ge(ga_ld, i * 32 + 16 * (24 + j + 1))
                        dve.wait_ge(cb_lo, 8)
                        dst = brow(acc, i * 2 + j)
                        for src, sl, q in parts(j):
                            gate = mod[:, bass.ds(i * 2 + (M_G1 + j), 1), q:q + 1].rearrange("p a b -> p (a b)")
                            x = dve.scalar_tensor_tensor(two(dst[:, sl], sl), src, gate, two(stage[1][:, sl], sl), ALU.mult, ALU.add)
                        x.then_inc(p_free[j], 1)
                        dve.wait_ge(sq_ok, i * 2 + (j + 1))
                        dve.tensor_tensor(ssq[:, :], ssq[:, :], stage[0][:, :], ALU.add).then_inc(sq_add, 1)
                invert(dve, 2)
                dve.wait_ge(rms_ok, 2)
                for k in range(KB + 1):
                    if k < KB:
                        if k >= 2:
                            dve.wait_ge(h2_lo, k - 1)
                        dve.tensor_tensor(stage[k % 2][:, :], acc[:, k, :], ssq[:, :], ALU.mult).then_inc(h2_t, 1)
                    if k >= 1:
                        dve.wait_ge(h2_hi, k)
                        dve.tensor_tensor(x0l[:, k - 1, :], stage[(k - 1) % 2][:, :], x0h[:, k - 1, :].bitcast(F32),
                                          ALU.subtract).then_inc(h2_lo, 1)
                dve.memset(ssq[:, :], 0.0).then_inc(sq_add, 1)
                with dve.Fori(0, 4) as i:
                    for j in range(8):
                        dve.wait_ge(p_free[j % 2], half(i, 16, U_MLP + j) + 1)
                        dve.tensor_tensor(stage[j % 2][:, :], stage[j % 2][:, :], stage[j % 2][:, :], ALU.mult).then_inc(m_sq, 1)
                        dve.wait_ge(m_hi, i * 8 + (j + 1))
                        dve.tensor_tensor(x1l[:, j, :], stage[j % 2][:, :], x1h[:, j, :].bitcast(F32), ALU.subtract).then_inc(m_lo, 1)
                    for j in range(8):
                        dve.wait_ge(p_full, unit_full(i, 16, U_MLP + 8 + j))
                        if j < 2:
                            dve.wait_ge(p_free[j], half(i, 16, U_MLP + j))
                        dst = acc[:, j, :]
                        for src, sl, q in parts(j % 2):
                            x = dve.scalar_tensor_tensor(two(dst[:, sl], sl), src, mod[:, M_G2 + j, q:q + 1],
                                                         two(dst[:, sl], sl), ALU.mult, ALU.add)
                        x.then_inc(p_free[j % 2], 1)
                dve.wait_ge(sq_ok, 16)
                dve.wait_ge(sq_add, 17)
                dve.tensor_tensor(ssq[:, :], ssq[:, :], stage[1][:, :], ALU.add).then_inc(sq_add, 1)
                dve.wait_ge(rms_sqrt, 7)
                dve.reciprocal(small[:, 48:48 + TT], small[:, 32:32 + TT]).then_inc(rms_ok, 1)
                dve.wait_ge(rms_ok, 3)
                for t in range(TT):
                    dve.wait_ge(o_trr, t + 1)
                    dve.tensor_scalar(ob[:, t, 512:D], ps[:, 3 + t % 3, :], small[:, 48 + t:49 + t], None, ALU.mult).then_inc(o_cpd, 1)

            @block.tensor
            def _(pe):
                for u0, ready, xh, xl in ((U_CONV, (c_lo, 1), x0h, x0l), (U_RET, (g_lo, 2), x1h, x1l),
                                          (U_RET + 8, (g_lo, 10), x0h, x0l), (U_OUT, (cb_lo, 1), x1h, x1l)):
                    if u0 == U_CONV:
                        unit_T(pe, 0, 2, u0, xh, xl, ready, pair=True)
                    with pe.Fori(1 if u0 == U_CONV else 0, 4) as i:
                        for j in range(2):
                            unit_T(pe, i, 2, u0 + j, xh, xl, ready)
                pe.wait_ge(sq_add, 9)
                pe.wait_ge(p_free[0], half(0, 16, U_MLP))
                mean_square(pe)
                pe.wait_ge(h2_t, 1)
                with pe.Fori(0, 4) as i:
                    for j in range(8):
                        unit_T(pe, i, 16, U_MLP + j, x0h, x0l, (h2_lo, 1))
                    for j in range(8):
                        unit_T(pe, i, 16, U_MLP + 8 + j, x1h, x1l, (m_lo, i * 8 + 3))

                def rows_of(t, b):
                    if t >= 3:
                        pe.wait_ge(o_cpa, t - 2) if b == 0 else pe.wait_ge(o_cpd, t - 2)
                    for k in range(4):
                        mm = pe.transpose(ps[:, 3 * b + t % 3, k * P:(k + 1) * P],
                                          fg[:, 4 * b + k, t * P:(t + 1) * P], ident[:, :])
                    mm.then_inc(o_trr if b else o_trl, 1)

                pe.wait_ge(p_free[0], half(3, 16, U_MLP + 14) + 1)
                pe.wait_ge(f_n, 4)
                for t in range(3):
                    rows_of(t, 0)
                pe.wait_ge(sq_add, 18)
                for t in range(TT):
                    mm = pe.matmul(ps[:, 6, t:t + 1], ssq[:, t * P:(t + 1) * P], ones_mean[:, 0:1], start=True, stop=True)
                mm.then_inc(rms_ps, 1)
                pe.wait_ge(p_free[1], half(3, 16, U_MLP + 15) + 1)
                pe.wait_ge(f_n, KB)
                for t in range(3):
                    rows_of(t, 1)
                for t in range(3, TT):
                    for b in (0, 1):
                        rows_of(t, b)


def shape_tables():
    p, x = np.arange(P, dtype=np.float32)[:, None], np.arange(GN, dtype=np.float32)[None, :]
    nf = DK // 4
    inv = np.float32(10000.0) ** (-np.arange(nf, dtype=np.float32) / np.float32(nf))
    tok = np.arange(T - P)
    ang = np.concatenate([(tok // GRID_W).astype(np.float32)[:, None] * inv,
                          (tok % GRID_W).astype(np.float32)[:, None] * inv], axis=-1).astype(np.float32)
    rope = np.zeros((P, 2, T), np.float32)
    rope[:, 0, :P] = 1.0
    rope[:, 0, P:] = np.cos(ang).T
    rope[:, 1, P:] = np.sin(ang).T
    c = 2 * P
    coef = np.stack([np.concatenate([p + 1, p + P + 1, c - 1 - p, P - 1 - p, 0 * p + c], 1),
                     np.concatenate([c - p, P - p, p, p + P, 0 * p + c], 1)], 1)
    d = (x - P) - p
    diff = np.stack([np.maximum(d, 0), d >= 0, np.maximum(-d, 0), d <= 0], 1)
    return {"ident": np.eye(P, dtype=np.float32), "rope": rope, "coef": coef.astype(np.float32),
            "diff": diff.astype(np.float32)}


_INS = ["x_prompt", "x_sample", "c", "state_ret", "c_ctx", "norm1_g", "norm2_g", "w_mod", "b_mod", "w_in",
        "conv_dw", "conv_b", "conv_norm_g", "w_conv_out", "ret_decay_logit", "w_ret_out", "w_out",
        "w_mlp1", "w_mlp2", "final_norm_g"]
_OUTS = [(1, 128, 1024), (1, 1024, 1024), (1, 1, 2, 4, 256, 512)]


def kernel(**inputs):
    import concourse.bacc as _bacc
    from concourse.bass_utils import run_bass_kernel_spmd as _run

    nc = _bacc.Bacc("TRN2", target_bir_lowering=False, num_devices=1, dynamic_dma_scratch_size=1024)
    arrays, args = {}, []
    given = {**{n: inputs[n] for n in _INS}, **shape_tables()}
    for name, a in given.items():
        arrays[f"in_{name}"] = np.ascontiguousarray(a)
        args.append(nc.dram_tensor(f"in_{name}", a.shape, F32, kind="ExternalInput").ap())
    for i, shape in enumerate(_OUTS):
        args.append(nc.dram_tensor(f"out_{i}", shape, F32, kind="ExternalOutput").ap())
    step_kernel(nc, *args)
    r = _run(nc, [arrays], core_ids=[0])
    return tuple(r.results[0][f"out_{i}"] for i in range(len(_OUTS)))
```
